# Optimizing a Trainium2 kernel written in Bass

```python
import math
import jax, jax.numpy as jnp
from jax import lax
import numpy as np

D_MODEL = 1024
BATCH = 1
SEQ = 512
DEPTH = 2

HEAD_DIM = 64
N_HEADS = D_MODEL // HEAD_DIM
N_KV_HEADS = 4
GRID_W = 64
NA_ROWS_MAX = 8
NA_COLS = 16
WINDOW = 128
BLOCK = 128
N_BUCKETS = 32
MAX_EXACT = 8
MAX_DISTANCE = 128
D_FF = 4 * D_MODEL
N_MIXERS = 2
N_A_LAYERS = (DEPTH + 1) // 2
N_B_LAYERS = DEPTH // 2
EPS = 1e-6

kernel_name = "hybrid_natten_swa_sqrelu_encoder"

def rms_norm(x, g):
    xf = x.astype(jnp.float32)
    y = xf * lax.rsqrt(jnp.mean(xf * xf, axis=-1, keepdims=True) + EPS)
    return (y * g.astype(jnp.float32)).astype(x.dtype)

def t5_bucket(rel):
    half = N_BUCKETS // 2
    rel = jnp.asarray(rel, dtype=jnp.int32)
    base = jnp.where(rel > 0, half, 0)
    n = jnp.abs(rel)
    nf = jnp.maximum(n, 1).astype(jnp.float32)
    large = MAX_EXACT + (jnp.log(nf / MAX_EXACT) / math.log(MAX_DISTANCE / MAX_EXACT)
                         * (half - MAX_EXACT)).astype(jnp.int32)
    large = jnp.minimum(large, half - 1)
    return base + jnp.where(n < MAX_EXACT, n, large)

def neighbourhood_attention(h, w_qkv, rpb, w_o):
    B, S, D = h.shape
    rows = S // GRID_W
    kr = min(NA_ROWS_MAX, rows)
    qkv = jnp.einsum('bsd,de->bse', h, w_qkv).reshape(B, rows, GRID_W, 3, N_HEADS, HEAD_DIM)
    q = qkv[..., 0, :, :] * (HEAD_DIM ** -0.5)
    k = qkv[..., 1, :, :]
    v = qkv[..., 2, :, :]
    cols = np.arange(GRID_W)
    col_start = np.clip(cols - NA_COLS // 2, 0, GRID_W - NA_COLS)
    col_idx = col_start[:, None] + np.arange(NA_COLS)[None, :]
    dc = col_idx - cols[:, None] + (NA_COLS - 1)
    rpb_c = rpb[:, :, dc]

    def row_block(args):
        r, q_r = args
        rs = jnp.clip(r - kr // 2, 0, rows - kr)
        k_rows = lax.dynamic_slice_in_dim(k, rs, kr, axis=1)
        v_rows = lax.dynamic_slice_in_dim(v, rs, kr, axis=1)
        k_win = k_rows[:, :, col_idx]
        v_win = v_rows[:, :, col_idx]
        s = jnp.einsum('bchd,brckhd->bhcrk', q_r, k_win).astype(jnp.float32)
        dr = rs + jnp.arange(kr) - r + (NA_ROWS_MAX - 1)
        bias = jnp.transpose(rpb_c[:, dr], (0, 2, 1, 3))
        s = s + bias[None].astype(jnp.float32)
        p = jax.nn.softmax(s.reshape(B, N_HEADS, GRID_W, kr * NA_COLS), axis=-1)
        p = p.reshape(B, N_HEADS, GRID_W, kr, NA_COLS).astype(v.dtype)
        return jnp.einsum('bhcrk,brckhd->bchd', p, v_win)

    q_rows = jnp.moveaxis(q, 1, 0)
    o = lax.map(row_block, (jnp.arange(rows), q_rows))
    o = jnp.moveaxis(o, 0, 1).reshape(B, S, D)
    return jnp.einsum('bsd,de->bse', o, w_o)

def sliding_window_gqa(h, w_qkv, sinks, rel_table, w_o):
    B, S, D = h.shape
    nb = S // BLOCK
    G = N_HEADS // N_KV_HEADS
    kvd = N_KV_HEADS * HEAD_DIM
    qkv = jnp.einsum('bsd,de->bse', h, w_qkv)
    q = qkv[..., :D].reshape(B, nb, BLOCK, N_KV_HEADS, G, HEAD_DIM) * (HEAD_DIM ** -0.5)
    k = qkv[..., D:D + kvd].reshape(B, S, N_KV_HEADS, HEAD_DIM)
    v = qkv[..., D + kvd:].reshape(B, S, N_KV_HEADS, HEAD_DIM)

    def band(t):
        tp = jnp.pad(t, ((0, 0), (BLOCK, BLOCK), (0, 0), (0, 0)))
        tp = tp.reshape(B, nb + 2, BLOCK, N_KV_HEADS, HEAD_DIM)
        return jnp.concatenate([tp[:, :-2], tp[:, 1:-1], tp[:, 2:]], axis=2)

    kb, vb = band(k), band(v)
    s = jnp.einsum('bnqhgd,bnjhd->bhgnqj', q, kb).astype(jnp.float32)
    rel = (np.arange(3 * BLOCK) - BLOCK)[None, :] - np.arange(BLOCK)[:, None]
    key_pos = np.arange(nb)[:, None] * BLOCK + np.arange(3 * BLOCK)[None, :] - BLOCK
    mask = (np.abs(rel) <= WINDOW)[None] & ((key_pos >= 0) & (key_pos < S))[:, None, :]
    bias = jnp.transpose(rel_table[t5_bucket(rel)], (2, 0, 1)).astype(jnp.float32)
    bias = bias.reshape(N_KV_HEADS, G, 1, BLOCK, 3 * BLOCK)
    s = jnp.where(jnp.asarray(mask), s + bias, jnp.finfo(jnp.float32).min)
    sink = sinks.astype(jnp.float32).reshape(1, N_KV_HEADS, G, 1, 1, 1)
    m = jnp.maximum(jnp.max(s, axis=-1, keepdims=True), sink)
    p = jnp.exp(s - m)
    p = p / (jnp.sum(p, axis=-1, keepdims=True) + jnp.exp(sink - m))
    o = jnp.einsum('bhgnqj,bnjhd->bnqhgd', p.astype(v.dtype), vb).reshape(B, S, D)
    return jnp.einsum('bsd,de->bse', o, w_o)

def squared_relu_mlp(h, w_in, w_out):
    u = jnp.square(jax.nn.relu(jnp.einsum('bsd,df->bsf', h, w_in)))
    return jnp.einsum('bsf,fd->bsd', u, w_out)

def setup_inputs(seed: int = 0) -> dict:
    key = jax.random.key(seed)
    ks = jax.random.split(key, 14)
    f32 = jnp.float32
    D = D_MODEL
    kvd = N_KV_HEADS * HEAD_DIM
    res_scale = (2 * DEPTH) ** -0.5
    return {
        "x": jax.random.normal(ks[0], (BATCH, SEQ, D), f32),
        "mix_norm": 1.0 + 0.01 * jax.random.normal(ks[1], (DEPTH, D), f32),
        "mlp_norm": 1.0 + 0.01 * jax.random.normal(ks[2], (DEPTH, D), f32),
        "final_norm": 1.0 + 0.01 * jax.random.normal(ks[3], (D,), f32),
        "na_w_qkv": jax.random.normal(ks[4], (N_A_LAYERS, D, 3 * D), f32) * D ** -0.5,
        "na_rpb": 0.1 * jax.random.normal(ks[5], (N_A_LAYERS, N_HEADS, 2 * NA_ROWS_MAX - 1, 2 * NA_COLS - 1), f32),
        "na_w_o": jax.random.normal(ks[6], (N_A_LAYERS, D, D), f32) * D ** -0.5 * res_scale,
        "swa_w_qkv": jax.random.normal(ks[7], (N_B_LAYERS, D, D + 2 * kvd), f32) * D ** -0.5,
        "swa_sinks": 0.5 * jax.random.normal(ks[8], (N_B_LAYERS, N_HEADS), f32),
        "swa_w_o": jax.random.normal(ks[9], (N_B_LAYERS, D, D), f32) * D ** -0.5 * res_scale,
        "t5_rel_table": 0.1 * jax.random.normal(ks[10], (N_BUCKETS, N_HEADS), f32),
        "mlp_w_in": jax.random.normal(ks[11], (DEPTH, D, D_FF), f32) * D ** -0.5,
        "mlp_w_out": jax.random.normal(ks[12], (DEPTH, D_FF, D), f32) * D_FF ** -0.5 * res_scale,
    }

def reference(x, mix_norm, mlp_norm, final_norm, na_w_qkv, na_rpb, na_w_o,
              swa_w_qkv, swa_sinks, swa_w_o, t5_rel_table, mlp_w_in, mlp_w_out):
    for i in range(DEPTH):
        j = i // N_MIXERS
        h = rms_norm(x, mix_norm[i])
        if i % N_MIXERS == 0:
            x = x + neighbourhood_attention(h, na_w_qkv[j], na_rpb[j], na_w_o[j])
        else:
            x = x + sliding_window_gqa(h, swa_w_qkv[j], swa_sinks[j], t5_rel_table, swa_w_o[j])
        h = rms_norm(x, mlp_norm[i])
        x = x + squared_relu_mlp(h, mlp_w_in[i], mlp_w_out[i])
    return rms_norm(x, final_norm)


_drawn_inputs = setup_inputs


def setup_inputs(seed=0):
    import zlib

    import numpy as np

    out = dict(_drawn_inputs(seed))
    spreads = {}
    factors = {'mix_norm': 8.0,
     'mlp_norm': 6.749,
     'final_norm': 36.432,
     'na_rpb': 7.66,
     'swa_sinks': 8.0,
     't5_rel_table': 33.43}
    for name, (base, spread) in spreads.items():
        noise = np.random.default_rng([zlib.crc32(name.encode()), seed]).standard_normal(out[name].shape)
        drawn = base * np.exp(spread * noise) if base else spread * noise
        out[name] = __import__('jax').numpy.asarray(drawn.astype(out[name].dtype))
    for name, factor in factors.items():
        out[name] = (out[name] * factor).astype(out[name].dtype)
    return out
```

```python
import numpy as np
from contextlib import ExitStack

import concourse.bass as bass
from concourse import mybir

F32 = mybir.dt.float32
F32R = mybir.dt.float32r
ALU = mybir.AluOpType
ACT = mybir.ActivationFunctionType

P = 128
D, SEQ, FF = 1024, 512, 4096
HD, HEADS, KV = 64, 16, 4
ROWS, COLS = 8, 64
NA_COLS = 16
KT = D // P
PAIRS = HEADS // 2
QT = SEQ // P
BLOCKS = 8
CHUNK = BLOCKS * P
HALF = FF // 2 // P
EPS = 1e-6
LOWEST = -3.0e38

QC = COLS // QT
WC = 32
WIN0 = [min(max(QC * j - NA_COLS // 2, 0), COLS - WC) for j in range(QT)]
U0 = [WIN0[j] - QC * j + NA_COLS for j in range(QT)]
BIASC = 48
RPB_R, RPB_C = 2 * ROWS - 1, 2 * NA_COLS - 1
PITCH = 64

SW_TILES = [[(0, 0, 2), (1, 0, 3)], [(3, 2, 2), (2, 1, 3)]]
BAND = 3 * P
RELS = 2 * P + 1
T5_W = P - QC + BAND
UNIT = 5 * P

CH_NA, CH_NAO, CH_MLP0 = 0, 24, 32
CH_SW, CH_SWO, CH_MLP1 = 96, 108, 116
CHUNKS = 180
GR_NA, GR_NAO, GR_MLP0, GR_SW, GR_SWO, GR_MLP1 = 0, 24, 32, 80, 92, 100
EARLY = 6
UNITS_NA = 2 * PAIRS
TI_NA, TI_MLP0, TI_SW, TI_MLP1 = 0, 16, 48, 58
NORMS = 5


class At:

    def __init__(self, a, b=0, i=None):
        self.a, self.b, self.i = a, b, i

    def __add__(self, n):
        return At(self.a + n, self.b, self.i)

    def __mul__(self, n):
        return At(self.a * n, self.b * n, self.i)

    @property
    def v(self):
        return self.a if self.i is None or self.b == 0 else self.i * self.b + self.a

    @property
    def half(self):
        return At(self.a // 2, self.b // 2, self.i)

    @property
    def odd(self):
        return self.a % 2


def encoder(nc, xT, wstream, gains, rpb, sinks, rel_table, na_mask, onehot, out):
    t5_dram = nc.dram_tensor("t5_shifted", (QC, HEADS, T5_W), F32, kind="Internal").ap()
    rpb_dram = nc.dram_tensor("rpb_shifted", (QC, HEADS, RPB_R, BIASC), F32, kind="Internal").ap()

    with ExitStack() as ctx:
        def sb(name, shape, dt=F32):
            return ctx.enter_context(nc.sbuf_tensor(name, shape, dt))

        def sem(name):
            return ctx.enter_context(nc.semaphore(name))

        x = sb("x_res", [P, KT, SEQ])
        h_hi, h_lo = sb("h_hi", [P, KT, SEQ], F32R), sb("h_lo", [P, KT, SEQ], F32R)
        w_raw = sb("w_raw", [P, 2, CHUNK])
        w_hi, w_lo = sb("w_hi", [P, 2, CHUNK], F32R), sb("w_lo", [P, 2, CHUNK], F32R)
        u_hi, u_lo = sb("u_hi", [P, HALF, SEQ], F32R), sb("u_lo", [P, HALF, SEQ], F32R)
        k_hi, k_lo = sb("k_hi", [P, 2, SEQ], F32R), sb("k_lo", [P, 2, SEQ], F32R)
        v_hi, v_lo = sb("v_hi", [P, 8, P], F32R), sb("v_lo", [P, 8, P], F32R)
        pt_hi, pt_lo = sb("pt_hi", [P, 8, P], F32R), sb("pt_lo", [P, 8, P], F32R)
        bias = sb("bias_all", [P, HEADS, BAND])
        probs = sb("probs", [P, 2 * UNIT])
        vT = sb("vT", [P, SEQ])
        bias_m = sb("bias_masked", [P, QT, WC, ROWS])
        onehot_sb = sb("onehot_sb", [32, RELS])
        sqsum = sb("sqsum", [P, SEQ])
        rstd = sb("rstd", [P, SEQ])
        scaled = sb("scaled", [P, 2, SEQ])
        ident, ones = sb("ident", [P, P]), sb("ones", [P, P])
        mask = sb("mask", [P, QT, WC])
        gain = sb("gain", [P, NORMS * KT])
        eps = sb("eps", [P, 1])
        sink, nsink = sb("sink", [P, HEADS]), sb("nsink", [P, HEADS])
        table = sb("table", [32, HEADS])
        nmax, rsum = sb("nmax", [P, 2, QT]), sb("rsum", [P, 2, QT])
        esink, rden = sb("esink", [P, 2, QT]), sb("rden", [P, 2, QT])
        rpb_pad = bias[0:HEADS, 0:3, :].rearrange("p a b -> p (a b)")[:, 0:RPB_R * PITCH]
        rpb_pad = rpb_pad.rearrange("p (r c) -> p r c", c=PITCH)
        t5_row = vT[0:HEADS, :]
        sw_bias = bias_m.rearrange("p a b c -> p (a b c)").rearrange("p (h n) -> p h n", h=2)
        sw_sink, sw_nsink = sb("sw_sink", [P, 2]), sb("sw_nsink", [P, 2])

        acc = [ctx.enter_context(nc.psum_tensor(f"acc{n}", [P, SEQ], F32)) for n in range(2)]
        s_ps = ctx.enter_context(nc.psum_tensor("s_ps", [P, 2, 512], F32))
        pt_ps = ctx.enter_context(nc.psum_tensor("pt_ps", [P, 8, P], F32))
        o_ps = ctx.enter_context(nc.psum_tensor("o_ps", [HD, SEQ], F32))
        misc_ps = ctx.enter_context(nc.psum_tensor("misc_ps", [P, QT, P], F32))

        w_landed = [sem("w_landed0"), sem("w_landed1")]
        x_landed = [sem(f"x_landed{k}") for k in range(KT)]
        gain_landed, consts_landed, table_landed = sem("gain_landed"), sem("consts_landed"), sem("table_landed")
        rpb_landed, rpb_stored, t5_stored = sem("rpb_landed"), sem("rpb_stored"), sem("t5_stored")
        na_bias_landed, t5_bias_landed, y_stored = sem("na_bias_landed"), sem("t5_bias_landed"), sem("y_stored")
        filled, pool_filled, ident_made = sem("filled"), sem("pool_filled"), sem("ident_made")
        t5_product, t5_cleared, t5_made = sem("t5_product"), sem("t5_cleared"), sem("t5_made")
        nsink_made = sem("nsink_made")
        w_hi_made, w_split, w_used = sem("w_hi_made"), sem("w_split"), sem("w_used")
        acc_taken = sem("acc_taken")
        squared, tile_hi, tile_split = sem("squared"), sem("tile_hi"), sem("tile_split")
        x_prepared, h_split, sq_cleared = sem("x_prepared"), sem("h_split"), sem("sq_cleared")
        stat_done, std_made, rstd_made = sem("stat_done"), sem("std_made"), sem("rstd_made")
        bias_made, logits_begun = sem("bias_made"), sem("logits_begun")
        scores_done, logits_made, probs_made = sem("scores_done"), sem("logits_made"), sem("probs_made")
        pt_done, pt_hi_made, pt_split, pv_done = sem("pt_done"), sem("pt_hi_made"), sem("pt_split"), sem("pv_done")
        probs_scaled = sem("probs_scaled")
        vt_done, v_hi_made, v_split = sem("vt_done"), sem("v_hi_made"), sem("v_split")
        den_made = sem("den_made")
        o_hi_made, o_split = sem("o_hi_made"), sem("o_split")
        y_made = sem("y_made")

        def f32(ap):
            return ap.bitcast(F32)

        def tokens(t):
            return t.rearrange("p (r c) -> p r c", c=COLS)

        def by_column(t):
            return t.rearrange("p (c r) -> p r c", r=ROWS)

        def in_tiles(t):
            return t.rearrange("p (j r c) -> p j r c", j=QT, c=QC)

        def by_tile(t):
            return t.rearrange("p (r j c) -> p j r c", j=QT, c=QC)

        def window(j):
            return slice(WIN0[j] * ROWS, (WIN0[j] + WC) * ROWS)

        def flat(t):
            return t.rearrange("p a b -> p (a b)")

        na_probs = probs[:, 0:QT * ROWS * WC].rearrange("p (j n) -> p j n", j=QT)

        def sw_probs(n, tile, blocks):
            at = (n % 2) * UNIT + 2 * P * tile
            return probs[:, at:at + blocks * P]

        def sw_before(p, n, by):
            return (p, n - by) if n >= by else (p + -1, n - by + 4)

        def sw_unit(p, n):
            return p * 4 + (UNITS_NA + n)

        block = ctx.enter_context(nc.Block())

        @block.sync
        def _(sp):
            def load_weights(c):
                if c.a >= 2 or c.b:
                    sp.wait_ge(w_split, (c + -1).v)
                sp.dma_start(w_raw[:, c.odd, :], wstream[c.v]).then_inc(w_landed[c.odd], 16)

            load_weights(At(0))
            sp.wait_ge(pool_filled, 2)
            sp.dma_start(rpb_pad[:, :, NA_COLS:NA_COLS + RPB_C], rpb).then_inc(rpb_landed, 16)
            load_weights(At(1))
            sp.wait_ge(rpb_landed, 16)
            for c in range(QC):
                sp.dma_start(rpb_dram[c], rpb_pad[:, :, QC - 1 - c:QC - 1 - c + BIASC]).then_inc(rpb_stored, 16)
            load_weights(At(2))
            load_weights(At(3))
            sp.wait_ge(rpb_stored, 16 * QC)
            for r in range(ROWS):
                sp.dma_start(bias[QC * r:QC * (r + 1), :, :],
                             rpb_dram[:, :, ROWS - 1 - r:RPB_R - r, :].rearrange("c h r u -> c h (r u)")
                             ).then_inc(na_bias_landed, 16)
            with sp.Fori(2, CHUNKS // 2) as i:
                for n in range(2):
                    load_weights(At(n, 2, i))
            for k in range(KT):
                sp.wait_ge(y_made, k + 1)
                sp.dma_start(out[k], x[:, k, :]).then_inc(y_stored, 16)
            sp.wait_ge(y_stored, 16 * KT)

        @block.gpsimd
        def _(pool):
            nc.gpsimd.memset(rpb_pad, 0.0).then_inc(pool_filled, 1)
            nc.gpsimd.memset(ident[:], 0.0).then_inc(pool_filled, 1)
            pool.wait_ge(pool_filled, 2)
            nc.gpsimd.affine_select(out=ident[:], in_=ident[:], compare_op=ALU.not_equal, fill=1.0, base=0,
                                    pattern=[[-1, P]], channel_multiplier=1).then_inc(ident_made, 1)
            pool.dma_start(mask[:], na_mask).then_inc(consts_landed, 16)
            pool.dma_start(table[:], rel_table).then_inc(table_landed, 16)
            pool.dma_start(onehot_sb[:], onehot).then_inc(table_landed, 16)
            pool.dma_start(sink[:], sinks.partition_broadcast(P)).then_inc(consts_landed, 16)
            pool.wait_ge(na_bias_landed, 16 * ROWS)
            pool.wait_ge(consts_landed, 16 * 2)

            def masked_bias(h):
                rows = bias[:, h.v, :].rearrange("p (r u) -> p r u", u=BIASC)
                for j in range(QT):
                    ins = nc.gpsimd.tensor_tensor(bias_m[:, j, :, :].rearrange("p c r -> p r c"),
                                                  rows[:, :, U0[j]:U0[j] + WC],
                                                  mask[:, j:j + 1, :].to_broadcast([P, ROWS, WC]), ALU.add)
                ins.then_inc(bias_made, 1)

            masked_bias(At(0))
            with pool.Fori(1, HEADS) as i:
                pool.wait_ge(logits_made, i)
                masked_bias(At(0, 1, i))
            pool.wait_ge(bias_made, HEADS)
            pool.wait_ge(t5_made, 1)
            for q in range(QC):
                pool.dma_start(t5_dram[q], t5_row[:, QC - 1 - q:QC - 1 - q + T5_W]).then_inc(t5_stored, 16)
            pool.wait_ge(t5_stored, 16 * QC)
            for a in range(P // QC):
                at = P - QC - QC * a
                pool.dma_start(bias[QC * a:QC * (a + 1), :, :], t5_dram[:, :, at:at + BAND]
                               ).then_inc(t5_bias_landed, 16)

            pool.wait_ge(nsink_made, 1)
            pool.wait_ge(t5_bias_landed, 16 * P // QC)

            def head_bias(pair, hh):
                head = pair * 2 + hh
                nc.gpsimd.tensor_copy(sw_bias[:, hh, 0:BAND], bias[:, head.v, :])
                nc.gpsimd.tensor_copy(sw_sink[:, hh:hh + 1], sink[:, bass.ds(head.v, 1)])
                nc.gpsimd.tensor_copy(sw_nsink[:, hh:hh + 1], nsink[:, bass.ds(head.v, 1)]).then_inc(bias_made, 1)

            pool.wait_ge(logits_made, UNITS_NA)
            head_bias(At(0), 0)
            head_bias(At(0), 1)
            with pool.Fori(1, PAIRS) as i:
                for hh in range(2):
                    pair = At(0, 1, i)
                    pool.wait_ge(probs_made, sw_unit(pair, 2 * hh - 2).v)
                    head_bias(pair, hh)

        @block.tensor
        def _(pe):
            def product(dst, a, b, start, stop):
                nc.tensor.matmul(dst, a[0], b[0], start=start, stop=False)
                nc.tensor.matmul(dst, a[0], b[1], start=False, stop=False)
                return nc.tensor.matmul(dst, a[1], b[0], start=False, stop=stop)

            def h_tile(k):
                return h_hi[:, k, :], h_lo[:, k, :]

            def u_tile(k):
                return u_hi[:, k, :], u_lo[:, k, :]

            def part(c, g, tile, ks, k0=0, first=True, last=True):
                if ks[0] == 0:
                    pe.wait_ge(w_split, (c + 1).v)
                    if first and g.a >= 2:
                        pe.wait_ge(acc_taken, (g + -1).v)
                for k in ks:
                    b = slice(k * P, (k + 1) * P)
                    ins = product(acc[g.odd][:], (w_hi[:, c.odd, b], w_lo[:, c.odd, b]), tile(k0 + k),
                                  first and k == 0, last and k == BLOCKS - 1)
                if ks[-1] == BLOCKS - 1:
                    ins.then_inc(w_used, 1)

            ALL = range(BLOCKS)

            def statistics(n):
                pe.wait_ge(h_split, KT * (n + 1))
                nc.tensor.matmul(flat(misc_ps[:]), ones[:], sqsum[:], start=True, stop=True).then_inc(stat_done, 1)

            def part_after_norm(c, g, n):
                for k in ALL:
                    pe.wait_ge(h_split, KT * n + k + 1)
                    if k == KT - 1:
                        statistics(n)
                    part(c, g, h_tile, [k])
                pe.wait_ge(std_made, n + 1)

            def transpose_v(blocks):
                for n, src in enumerate(blocks):
                    ins = nc.tensor.transpose(misc_ps[:, n, :], src, ident[:])
                ins.then_inc(vt_done, 1)

            def na_scores(p, hh):
                unit = p * 2 + hh
                if unit.a >= 1:
                    pe.wait_ge(logits_made, unit.v)
                s, q = slice(HD * hh, HD * (hh + 1)), 8 + p.odd
                for j in range(QT):
                    qs, ks = slice(P * j, P * (j + 1)), window(j)
                    ins = product(s_ps[:, j // 2, 256 * (j % 2):256 * (j % 2 + 1)],
                                  (u_hi[s, q, qs], u_lo[s, q, qs]),
                                  (k_hi[s, p.odd, ks], k_lo[s, p.odd, ks]), True, True)
                ins.then_inc(scores_done, 1)

            def na_transpose(p, hh):
                unit = p * 2 + hh
                pe.wait_ge(probs_scaled, (unit + 1).v)
                if unit.a >= 1:
                    pe.wait_ge(pt_split, unit.v)
                for j in range(QT):
                    for b in range(2):
                        ins = nc.tensor.transpose(pt_ps[:, 2 * j + b, :], na_probs[:, j, b * P:(b + 1) * P],
                                                  ident[:])
                ins.then_inc(pt_done, 1)

            def na_values(p, hh):
                head = p * 2 + hh
                pe.wait_ge(pt_split, (head + 1).v)
                pe.wait_ge(v_split, (p * 2 + 2).v)
                if head.a >= 1:
                    pe.wait_ge(o_split, head.v)
                s = slice(HD * hh, HD * (hh + 1))
                for j in range(QT):
                    for b in range(2):
                        n = 2 * j + b
                        ins = product(o_ps[:, P * j:P * (j + 1)], (v_hi[:, n, s], v_lo[:, n, s]),
                                      (pt_hi[:, n, :], pt_lo[:, n, :]), b == 0, b == 1)
                ins.then_inc(pv_done, 1)

            def na_v_blocks(p, batch):
                if batch == 0:
                    pe.wait_ge(acc_taken, (p * 3 + (GR_NA + 3)).v)
                    if p.a >= 1:
                        pe.wait_ge(v_split, (p * 2).v)
                else:
                    pe.wait_ge(v_split, (p * 2 + 1).v)
                transpose_v([vT[:, window(2 * batch + j)][:, P * b:P * (b + 1)] for j in range(2) for b in range(2)])

            def na_step(m, dense=True, attend=True):
                p, c, g = m + -1, m * 3 + CH_NA, m * 3 + GR_NA

                def dense_part(n):
                    if dense and m.a == 0 and n == 0:
                        part_after_norm(c, g, 0)
                    elif dense:
                        part(c + n, g + n, h_tile, ALL)
                    elif n < 2:
                        pe.wait_ge(o_split, 2 * EARLY)
                        part(At(CH_NAO + n), At(GR_NAO + n), u_tile, range(EARLY))

                if attend:
                    pe.wait_ge(tile_split, (p * 2 + (TI_NA + 2)).v)
                    na_scores(p, 0)
                    na_v_blocks(p, 0)
                dense_part(0)
                if attend:
                    na_transpose(p, 0)
                    na_v_blocks(p, 1)
                    na_scores(p, 1)
                dense_part(1)
                if attend:
                    na_values(p, 0)
                    na_transpose(p, 1)
                dense_part(2)
                if attend:
                    na_values(p, 1)

            def output_projection(ch, gr, heads_before):
                for n in range(2):
                    for k in range(EARLY, KT):
                        pe.wait_ge(o_split, heads_before + 2 * (k + 1))
                        part(At(ch + n), At(gr + n), u_tile, [k])
                with pe.Fori(0, 3) as i:
                    for n in range(2):
                        part(At(ch + 2 + n, 2, i), At(gr + 2 + n, 2, i), u_tile, ALL)

            def mlp(ch, gr, ti, norm):
                for half in range(2):
                    c0, g0 = ch + 32 * half, gr + 24 * half
                    start = 0
                    if half == 0:
                        part_after_norm(At(c0), At(g0), norm)
                        part(At(c0 + 1), At(g0 + 1), h_tile, ALL)
                        start = 1
                    with pe.Fori(start, HALF // 2) as i:
                        for n in range(2):
                            part(At(c0 + n, 2, i), At(g0 + n, 2, i), h_tile, ALL)
                    split = ti + HALF * half
                    with pe.Fori(0, KT // 2) as i:
                        for n in range(2):
                            c, g = At(c0 + HALF + 2 * n, 4, i), At(g0 + HALF + n, 2, i)
                            pe.wait_ge(tile_split, split + BLOCKS)
                            part(c, g, u_tile, ALL, 0, True, False)
                            pe.wait_ge(tile_split, split + HALF - 2)
                            part(c + 1, g, u_tile, range(6), BLOCKS, False, True)
                            pe.wait_ge(tile_split, split + HALF)
                            part(c + 1, g, u_tile, range(6, BLOCKS), BLOCKS, False, True)

            def sw_scores(p, n):
                hh = n // 2
                pe.wait_ge(logits_made, sw_unit(p, n).v)
                s, q, kv = slice(HD * hh, HD * (hh + 1)), 8 + p.odd, p.odd
                for tile, (i, kb, nb) in enumerate(SW_TILES[n % 2]):
                    qs, ks = slice(P * i, P * (i + 1)), slice(P * kb, P * (kb + nb))
                    ins = product(s_ps[:, tile, 0:nb * P], (u_hi[s, q, qs], u_lo[s, q, qs]),
                                  (k_hi[s, kv, ks], k_lo[s, kv, ks]), True, True)
                ins.then_inc(scores_done, 1)

            def sw_transpose(p, n):
                unit = sw_unit(p, n)
                pe.wait_ge(probs_scaled, (unit + 1).v)
                pe.wait_ge(pt_split, unit.v)
                at = 0
                for tile, (i, kb, nb) in enumerate(SW_TILES[n % 2]):
                    for b in range(nb):
                        ins = nc.tensor.transpose(pt_ps[:, at, :], sw_probs(n, tile, nb)[:, b * P:(b + 1) * P],
                                                  ident[:])
                        at += 1
                ins.then_inc(pt_done, 1)

            def sw_values(p, n):
                hh, kv, at = n // 2, p.odd, 0
                pe.wait_ge(pt_split, (sw_unit(p, n) + 1).v)
                if n % 2 == 0:
                    pe.wait_ge(o_split, (p * 2 + (HEADS + hh)).v)
                s = slice(HD * hh, HD * (hh + 1))
                for i, kb, nb in SW_TILES[n % 2]:
                    for b in range(nb):
                        v = 4 * kv + kb + b
                        ins = product(o_ps[:, P * i:P * (i + 1)], (v_hi[:, v, s], v_lo[:, v, s]),
                                      (pt_hi[:, at, :], pt_lo[:, at, :]), b == 0, b == nb - 1)
                        at += 1
                ins.then_inc(pv_done, 1)

            def sw_v_blocks(kv):
                pe.wait_ge(acc_taken, GR_SW + 2 * kv + 2)
                if kv:
                    pe.wait_ge(v_split, UNITS_NA + 1)
                transpose_v([vT[:, b * P:(b + 1) * P] for b in range(QT)])

            def sw_step(m, before=True, last=None):
                p, c, g = m + -1, m + (CH_SW + 4), m + (GR_SW + 4)

                def dense_part(n):
                    if last == 8:
                        if n == 0:
                            pe.wait_ge(o_split, HEADS + 2 * EARLY)
                        t = n + 4
                        part(At(CH_SWO + t // EARLY), At(GR_SWO + t // EARLY), u_tile, [t % EARLY])
                    elif n < 4:
                        part(c, g, h_tile, [4 + n])
                    else:
                        part(c + 1, g + 1, u_tile if last == 7 else h_tile, [n - 4])

                pe.wait_ge(tile_split, (p + (TI_SW + 3)).v)
                for n in range(4):
                    sw_scores(p, n)
                    dense_part(2 * n)
                    if before or n >= 2:
                        sw_values(*sw_before(p, n, 2))
                    if before or n >= 1:
                        sw_transpose(*sw_before(p, n, 1))
                    dense_part(2 * n + 1)

            pe.wait_ge(filled, 1)
            pe.wait_ge(ident_made, 1)
            na_step(At(0), attend=False)
            na_step(At(1))
            with pe.Fori(0, 3) as i:
                for n in range(2):
                    na_step(At(2 + n, 2, i))
            na_step(At(8), dense=False)
            pe.wait_ge(table_landed, 16 * 2)
            pe.wait_ge(logits_made, UNITS_NA)
            nc.tensor.matmul(s_ps[0:HEADS, 0, 0:RELS], table[:], onehot_sb[:], start=True,
                             stop=True).then_inc(t5_product, 1)
            output_projection(CH_NAO, GR_NAO, 0)
            mlp(CH_MLP0, GR_MLP0, TI_MLP0, 1)
            part_after_norm(At(CH_SW), At(GR_SW), 2)
            part(At(CH_SW + 1), At(GR_SW + 1), h_tile, ALL)
            part(At(CH_SW + 2), At(GR_SW + 2), h_tile, ALL)
            sw_v_blocks(0)
            part(At(CH_SW + 3), At(GR_SW + 3), h_tile, ALL)
            part(At(CH_SW + 4), At(GR_SW + 4), h_tile, ALL)
            sw_v_blocks(1)
            part(At(CH_SW + 5), At(GR_SW + 5), h_tile, range(4))
            pe.wait_ge(v_split, UNITS_NA + 2)
            pe.wait_ge(t5_made, 1)
            sw_step(At(1), before=False)
            with pe.Fori(0, 2) as i:
                for n in range(2):
                    sw_step(At(2 + n, 2, i))
            sw_step(At(6))
            sw_step(At(7), last=7)
            sw_step(At(8), last=8)
            sw_values(At(7), 2)
            sw_transpose(At(7), 3)
            sw_values(At(7), 3)
            output_projection(CH_SWO, GR_SWO, HEADS)
            mlp(CH_MLP1, GR_MLP1, TI_MLP1, 3)
            statistics(4)

        @block.scalar
        def _(act):
            def split_weights(c):
                if c.a >= 2:
                    act.wait_ge(w_used, (c + -1).v)
                act.wait_ge(w_landed[c.odd], ((c.half + 1) * 16).v)
                nc.scalar.copy(w_hi[:, c.odd, :], w_raw[:, c.odd, :]).then_inc(w_hi_made, 1)

            def prepare_x(n, k, landed):
                tile = k + KT * n
                landed()
                if tile.a >= 2:
                    act.wait_ge(h_split, (tile + -1).v)
                act.wait_ge(gain_landed, 16)
                if n < NORMS - 1:
                    nc.scalar.activation(h_hi[:, k.v, :], x[:, k.v, :], ACT.Copy, scale=gain_of(n, k))
                nc.scalar.activation(probs[:, SEQ * k.odd:SEQ * (k.odd + 1)], x[:, k.v, :],
                                     ACT.Square).then_inc(x_prepared, 1)

            def gain_of(n, k):
                at = k + KT * n
                return gain[:, bass.ds(at.v, 1)]

            def deviation(n):
                act.wait_ge(stat_done, n + 1)
                nc.scalar.activation(rstd[:], flat(misc_ps[:]), ACT.Sqrt, bias=eps[:], scale=1.0 / D
                                     ).then_inc(std_made, 1)

            def tile_high(g, e, dst, square=None, order=None):
                act.wait_ge(acc_taken, (g + 1).v)
                src = scaled[:, e.odd, :]
                if square is not None:
                    nc.scalar.activation(src, src, ACT.Square).then_inc(squared, 1)
                    act.wait_ge(squared, (square + 1).v)
                if order is not None:
                    dst, src = order[0](dst), order[1](src)
                nc.scalar.copy(dst, src).then_inc(tile_hi, 1)

            def v_high(batch, dst):
                act.wait_ge(vt_done, (batch + 1).v)
                nc.scalar.copy(dst, misc_ps[:]).then_inc(v_hi_made, 1)

            def exponent(src, slot, i):
                return nc.scalar.activation(src, src, ACT.Exp, bias=nmax[:, slot, i:i + 1], scale=-1.0,
                                            accum_out=rsum[:, slot, i:i + 1])

            def pt_high(unit, blocks):
                act.wait_ge(pt_done, (unit + 1).v)
                nc.scalar.copy(pt_hi[:, 0:blocks, :], pt_ps[:, 0:blocks, :]).then_inc(pt_hi_made, 1)

            def o_high(unit, head, tile, hh, grid):
                act.wait_ge(pv_done, (unit + 1).v)
                dst, src = u_hi[HD * hh:HD * (hh + 1), tile.v, :], o_ps[:, :]
                if grid:
                    dst, src = by_tile(dst), in_tiles(src)
                nc.scalar.copy(dst, src).then_inc(o_hi_made, 1)

            def na_exp(p, hh):
                unit = p * 2 + hh
                act.wait_ge(logits_made, (unit + 1).v)
                for j in range(QT):
                    ins = exponent(na_probs[:, j, :], hh, j)
                ins.then_inc(probs_made, 1)

            def na_step(m, dense=True, attend=True):
                p, c, g = m + -1, m * 3 + CH_NA, m * 3 + GR_NA
                if attend:
                    v_high(p * 2, v_hi[:, 0:4, :])
                    na_exp(p, 0)
                if dense:
                    split_weights(c + 2)
                    if m.a == 0:
                        deviation(0)
                    tile_high(g, m * 2 + TI_NA, u_hi[:, 8 + m.odd, :], order=(in_tiles, by_tile))
                if attend:
                    pt_high(p * 2, 8)
                    v_high(p * 2 + 1, v_hi[:, 4:8, :])
                    na_exp(p, 1)
                if dense:
                    split_weights(c + 3)
                    tile_high(g + 1, m * 2 + (TI_NA + 1), k_hi[:, m.odd, :], order=(by_column, tokens))
                if attend:
                    pt_high(p * 2 + 1, 8)
                    o_high(p * 2, p * 2, p, 0, True)
                if dense:
                    split_weights(c + 4)
                if attend:
                    o_high(p * 2 + 1, p * 2 + 1, p, 1, True)

            def output_projection(ch, gr, norm):
                with act.Fori(0, KT // 2) as i:
                    for n in range(2):
                        g = At(gr + n, 2, i)
                        split_weights(At(ch + n + 2, 2, i))
                        prepare_x(norm, At(n, 2, i), lambda: act.wait_ge(acc_taken, (g + 1).v))

            def mlp(ch, gr, ti, sq, norm):
                for half in range(2):
                    c0, g0 = ch + 32 * half, gr + 24 * half
                    split_weights(At(c0 + 2))
                    if half == 0:
                        deviation(norm)

                    def hidden(n, i, first=False):
                        f = At(n, 2, i) if i is not None else At(n)
                        if not first:
                            split_weights(f + (c0 + 2))
                        tile_high(f + g0, f + (ti + HALF * half), u_hi[:, f.v, :], f + (sq + HALF * half))

                    hidden(0, None, True)
                    hidden(1, None)
                    with act.Fori(1, HALF // 2) as i:
                        hidden(0, i)
                        hidden(1, i)

                    def down(n, i):
                        m = At(n, 2, i) if i is not None else At(n)
                        g = m + (g0 + HALF)
                        c = m * 2 + (c0 + HALF + 2)
                        for t in range(2):
                            if (c + t).a < CHUNKS:
                                split_weights(c + t)
                        if half == 1:
                            prepare_x(norm + 1, m, lambda: act.wait_ge(acc_taken, (g + 1).v))

                    with act.Fori(0, KT // 2 - 1) as i:
                        down(0, i)
                        down(1, i)
                    down(KT - 2, None)
                    down(KT - 1, None)

            def sw_exp(p, n):
                unit, hh = sw_unit(p, n), n // 2
                act.wait_ge(logits_made, (unit + 1).v)
                for tile, (i, kb, nb) in enumerate(SW_TILES[n % 2]):
                    exponent(sw_probs(n, tile, nb), n % 2, tile)
                nc.scalar.activation(esink[:, n % 2, 0:2], nmax[:, n % 2, 0:2], ACT.Exp, bias=sw_sink[:, hh:hh + 1]
                                     ).then_inc(probs_made, 1)

            def sw_pt_high(p, n):
                pt_high(sw_unit(p, n), UNIT // P)

            def sw_o_high(p, hh):
                o_high(sw_unit(p, 2 * hh + 1), p * 2 + (HEADS + hh), p, hh, False)

            def sw_step(m, before=True, dense=True):
                p = m + -1
                for n in range(4):
                    sw_exp(p, n)
                    if before or n >= 1:
                        sw_pt_high(*sw_before(p, n, 1))
                    if n == 1 and before:
                        sw_o_high(p + -1, 1)
                    if n == 1 and dense:
                        split_weights(m + (CH_SW + 6))
                        tile_high(m + (GR_SW + 4), m + (TI_SW + 2), u_hi[:, 8 + m.odd, :])
                sw_o_high(p, 0)

            act.dma_start(gain[:], gains).then_inc(gain_landed, 16)
            for k in range(KT):
                act.dma_start(x[:, k, :], xT[k]).then_inc(x_landed[k], 16)
            for k in range(KT):
                prepare_x(0, At(k), lambda: act.wait_ge(x_landed[k], 16))
                if k < 2:
                    split_weights(At(k))
            act.wait_ge(filled, 2)
            na_step(At(0), attend=False)
            na_step(At(1))
            with act.Fori(0, 3) as i:
                for n in range(2):
                    na_step(At(2 + n, 2, i))
            na_step(At(8), dense=False)
            output_projection(CH_NAO, GR_NAO, 1)
            mlp(CH_MLP0, GR_MLP0, TI_MLP0, 0, 1)
            split_weights(At(CH_SW + 2))
            deviation(2)
            tile_high(At(GR_SW), At(TI_SW), k_hi[:, 0, :])
            split_weights(At(CH_SW + 3))
            split_weights(At(CH_SW + 4))
            tile_high(At(GR_SW + 2), At(TI_SW + 1), k_hi[:, 1, :])
            v_high(At(UNITS_NA), v_hi[:, 0:4, :])
            split_weights(At(CH_SW + 5))
            split_weights(At(CH_SW + 6))
            tile_high(At(GR_SW + 4), At(TI_SW + 2), u_hi[:, 8, :])
            v_high(At(UNITS_NA + 1), v_hi[:, 4:8, :])
            sw_step(At(1), before=False)
            with act.Fori(0, 3) as i:
                for n in range(2):
                    sw_step(At(2 + n, 2, i))
            sw_step(At(8), dense=False)
            sw_pt_high(At(7), 3)
            sw_o_high(At(7), 1)
            output_projection(CH_SWO, GR_SWO, 3)
            mlp(CH_MLP1, GR_MLP1, TI_MLP1, 32, 3)
            deviation(4)

        @block.vector
        def _(dve):
            def split_weights(c):
                dve.wait_ge(w_hi_made, (c + 1).v)
                nc.vector.tensor_tensor(w_lo[:, c.odd, :], w_raw[:, c.odd, :], f32(w_hi[:, c.odd, :]),
                                        ALU.subtract).then_inc(w_split, 1)

            def clear_squares(n):
                nc.vector.memset(sqsum[:], 0.0).then_inc(sq_cleared, 1)

            def finish_x(n, k):
                tile = k + KT * n
                dve.wait_ge(x_prepared, (tile + 1).v)
                if n < NORMS - 1:
                    nc.vector.scalar_tensor_tensor(out=h_lo[:, k.v, :], in0=x[:, k.v, :],
                                                   scalar=gain[:, bass.ds(tile.v, 1)], in1=f32(h_hi[:, k.v, :]),
                                                   op0=ALU.mult, op1=ALU.subtract)
                dve.wait_ge(sq_cleared, n + 1)
                if tile.a >= 1:
                    dve.wait_ge(h_split, tile.v)
                nc.vector.tensor_tensor(sqsum[:], sqsum[:], probs[:, SEQ * k.odd:SEQ * (k.odd + 1)],
                                        ALU.add).then_inc(h_split, 1)

            def reciprocal_deviation(n):
                dve.wait_ge(std_made, n + 1)
                nc.vector.reciprocal(rstd[:], rstd[:]).then_inc(rstd_made, 1)
                dve.wait_ge(rstd_made, n + 1)

            def scale(c, g, dst, factor, op=ALU.mult, order=lambda t: t):
                dve.wait_ge(w_used, (c + 1).v)
                nc.vector.scalar_tensor_tensor(out=dst, in0=order(acc[g.odd][:]), scalar=factor,
                                               in1=order(rstd[:]), op0=op, op1=ALU.mult).then_inc(acc_taken, 1)

            def scale_tile(c, g, e, factor, op=ALU.mult):
                if e.a >= 2:
                    dve.wait_ge(tile_split, (e + -1).v)
                scale(c, g, scaled[:, e.odd, :], factor, op)

            def tile_low(e, dst, hi, order=(lambda t: t, lambda t: t)):
                dve.wait_ge(tile_hi, (e + 1).v)
                nc.vector.tensor_tensor(order[0](dst), order[1](scaled[:, e.odd, :]), order[0](f32(hi)),
                                        ALU.subtract).then_inc(tile_split, 1)

            def v_low(batch, s):
                dve.wait_ge(v_hi_made, (batch + 1).v)
                nc.vector.tensor_tensor(v_lo[:, s, :], misc_ps[:], f32(v_hi[:, s, :]),
                                        ALU.subtract).then_inc(v_split, 1)

            def pt_low(unit, blocks):
                dve.wait_ge(pt_hi_made, (unit + 1).v)
                nc.vector.tensor_tensor(pt_lo[:, 0:blocks, :], pt_ps[:, 0:blocks, :], f32(pt_hi[:, 0:blocks, :]),
                                        ALU.subtract).then_inc(pt_split, 1)

            def o_low(head, tile, hh, grid):
                dve.wait_ge(o_hi_made, (head + 1).v)
                s = slice(HD * hh, HD * (hh + 1))
                hi, lo, src = f32(u_hi[s, tile.v, :]), u_lo[s, tile.v, :], o_ps[:, :]
                if grid:
                    hi, lo, src = by_tile(hi), by_tile(lo), in_tiles(src)
                nc.vector.tensor_tensor(lo, src, hi, ALU.subtract).then_inc(o_split, 1)

            def logits(dst, scores, add, start, slot, i):
                return nc.vector.tensor_tensor_reduce(out=dst, in0=scores, in1=add, scale=-1.0, scalar=start,
                                                      op0=ALU.add, op1=ALU.min, accum_out=nmax[:, slot, i:i + 1])

            def na_logits(p, hh):
                unit = p * 2 + hh
                dve.wait_ge(scores_done, (unit + 1).v)
                dve.wait_ge(bias_made, (unit + 1).v)
                if unit.a >= 1:
                    dve.wait_ge(pt_done, unit.v)
                dve.sem_inc(logits_begun, 1)
                for j in range(QT):
                    ins = logits(na_probs[:, j, :], s_ps[:, j // 2, 256 * (j % 2):256 * (j % 2 + 1)],
                                 bias_m[:, j, :, :].rearrange("p c r -> p (c r)"), -LOWEST, hh, j)
                ins.then_inc(logits_made, 1)

            def na_scale_probs(p, hh):
                unit = p * 2 + hh
                dve.wait_ge(probs_made, (unit + 1).v)
                nc.vector.reciprocal(rden[:, hh, :], rsum[:, hh, :]).then_inc(den_made, 1)
                dve.wait_ge(den_made, (unit + 1).v)
                for j in range(QT):
                    ins = nc.vector.tensor_scalar(na_probs[:, j, :], na_probs[:, j, :], rden[:, hh, j:j + 1], None,
                                                  ALU.mult)
                ins.then_inc(probs_scaled, 1)

            def na_step(m, dense=True, attend=True):
                p, c, g = m + -1, m * 3 + CH_NA, m * 3 + GR_NA
                if attend:
                    na_logits(p, 0)
                    v_low(p * 2, slice(0, 4))
                    na_scale_probs(p, 0)
                if dense:
                    if m.a == 0:
                        reciprocal_deviation(0)
                    e = m * 2 + TI_NA
                    scale_tile(c, g, e, HD ** -0.5)
                    split_weights(c + 2)
                    tile_low(e, u_lo[:, 8 + m.odd, :], u_hi[:, 8 + m.odd, :], (in_tiles, by_tile))
                if attend:
                    pt_low(p * 2, 8)
                    v_low(p * 2 + 1, slice(4, 8))
                    na_logits(p, 1)
                    na_scale_probs(p, 1)
                if dense:
                    e = m * 2 + (TI_NA + 1)
                    scale_tile(c + 1, g + 1, e, 1.0)
                    split_weights(c + 3)
                    tile_low(e, k_lo[:, m.odd, :], k_hi[:, m.odd, :], (by_column, tokens))
                if attend:
                    pt_low(p * 2 + 1, 8)
                    o_low(p * 2, p, 0, True)
                if dense:
                    scale(c + 2, g + 2, by_column(vT[:, :]), 1.0, order=tokens)
                    split_weights(c + 4)
                if attend:
                    o_low(p * 2 + 1, p, 1, True)

            def add_to_x(c, g, k):
                dve.wait_ge(w_used, (c + 1).v)
                nc.vector.tensor_tensor(x[:, k.v, :], acc[g.odd][:], x[:, k.v, :], ALU.add).then_inc(acc_taken, 1)

            def output_projection(ch, gr, norm):
                with dve.Fori(0, KT // 2) as i:
                    for n in range(2):
                        c = At(ch + n, 2, i)
                        add_to_x(c, At(gr + n, 2, i), At(n, 2, i))
                        split_weights(c + 2)
                        finish_x(norm, At(n, 2, i))

            def mlp(ch, gr, ti, norm):
                for half in range(2):
                    c0, g0 = ch + 32 * half, gr + 24 * half
                    if half == 0:
                        reciprocal_deviation(norm)
                    with dve.Fori(0, HALF // 2) as i:
                        for n in range(2):
                            f = At(n, 2, i)
                            e = f + (ti + HALF * half)
                            scale_tile(f + c0, f + g0, e, 0.0, ALU.max)
                            split_weights(f + (c0 + 2))
                            tile_low(e, u_lo[:, f.v, :], u_hi[:, f.v, :])
                    if half == 1:
                        clear_squares(norm + 1)

                    def down(n, i):
                        m = At(n, 2, i) if i is not None else At(n)
                        c = m * 2 + (c0 + HALF)
                        if (c + 2).a < CHUNKS:
                            split_weights(c + 2)
                        add_to_x(c + 1, m + (g0 + HALF), m)
                        if (c + 3).a < CHUNKS:
                            split_weights(c + 3)
                        if half == 1:
                            finish_x(norm + 1, m)

                    with dve.Fori(0, KT // 2 - 1) as i:
                        down(0, i)
                        down(1, i)
                    down(KT - 2, None)
                    down(KT - 1, None)

            def sw_logits(p, n):
                unit, hh = sw_unit(p, n), n // 2
                head = p * 2 + hh
                dve.wait_ge(scores_done, (unit + 1).v)
                dve.wait_ge(bias_made, (head + (HEADS + 1)).v)
                dve.wait_ge(pt_done, (unit + -1).v)
                dve.sem_inc(logits_begun, 1)
                for tile, (i, kb, nb) in enumerate(SW_TILES[n % 2]):
                    at = (kb - i + 1) * P
                    ins = logits(sw_probs(n, tile, nb), s_ps[:, tile, 0:nb * P], sw_bias[:, hh, at:at + nb * P],
                                 sw_nsink[:, hh:hh + 1], n % 2, tile)
                ins.then_inc(logits_made, 1)

            def sw_scale_probs(p, n):
                unit, slot = sw_unit(p, n), n % 2
                dve.wait_ge(probs_made, (unit + 1).v)
                nc.vector.tensor_tensor(rden[:, slot, 0:2], rsum[:, slot, 0:2], esink[:, slot, 0:2],
                                        ALU.add).then_inc(den_made, 1)
                dens = p * 8 + (UNITS_NA + 2 * n)
                dve.wait_ge(den_made, (dens + 1).v)
                nc.vector.reciprocal(rden[:, slot, 0:2], rden[:, slot, 0:2]).then_inc(den_made, 1)
                dve.wait_ge(den_made, (dens + 2).v)
                for tile, (i, kb, nb) in enumerate(SW_TILES[n % 2]):
                    t = sw_probs(n, tile, nb)
                    ins = nc.vector.tensor_scalar(t, t, rden[:, slot, tile:tile + 1], None, ALU.mult)
                ins.then_inc(probs_scaled, 1)

            def sw_pt_low(p, n):
                pt_low(sw_unit(p, n), UNIT // P)

            def sw_o_low(p, hh):
                o_low(p * 2 + (HEADS + hh), p, hh, False)

            def queries(m):
                c, e = m + (CH_SW + 4), m + (TI_SW + 2)
                scale_tile(c, m + (GR_SW + 4), e, HD ** -0.5)
                split_weights(c + 2)
                tile_low(e, u_lo[:, 8 + m.odd, :], u_hi[:, 8 + m.odd, :])

            def sw_step(m, before=True, dense=True):
                p = m + -1
                for n in range(4):
                    sw_logits(p, n)
                    sw_scale_probs(p, n)
                    if before or n >= 1:
                        sw_pt_low(*sw_before(p, n, 1))
                    if n == 1 and before:
                        sw_o_low(p + -1, 1)
                    if n == 1 and dense:
                        queries(m)
                sw_o_low(p, 0)

            nc.vector.memset(ones[:], 1.0).then_inc(filled, 1)
            nc.vector.memset(eps[:], EPS).then_inc(filled, 1)
            clear_squares(0)
            dve.wait_ge(gain_landed, 16)
            for k in range(KT):
                finish_x(0, At(k))
                if k < 2:
                    split_weights(At(k))
            na_step(At(0), attend=False)
            dve.wait_ge(consts_landed, 16 * 2)
            nc.vector.tensor_scalar(nsink[:], sink[:], -1.0, None, ALU.mult).then_inc(nsink_made, 1)
            na_step(At(1))
            with dve.Fori(0, 3) as i:
                for n in range(2):
                    na_step(At(2 + n, 2, i))
            na_step(At(8), dense=False)
            nc.vector.memset(t5_row, LOWEST).then_inc(t5_cleared, 1)
            dve.wait_ge(t5_cleared, 1)
            dve.wait_ge(t5_product, 1)
            nc.vector.tensor_copy(t5_row[:, P - 1:P - 1 + RELS], s_ps[0:HEADS, 0, 0:RELS]).then_inc(t5_made, 1)
            clear_squares(1)
            output_projection(CH_NAO, GR_NAO, 1)
            mlp(CH_MLP0, GR_MLP0, TI_MLP0, 1)
            reciprocal_deviation(2)
            scale_tile(At(CH_SW), At(GR_SW), At(TI_SW), 1.0)
            split_weights(At(CH_SW + 2))
            tile_low(At(TI_SW), k_lo[:, 0, :], k_hi[:, 0, :])
            dve.wait_ge(t5_stored, 16 * QC)
            scale(At(CH_SW + 1), At(GR_SW + 1), vT[:, :], 1.0)
            split_weights(At(CH_SW + 3))
            scale_tile(At(CH_SW + 2), At(GR_SW + 2), At(TI_SW + 1), 1.0)
            split_weights(At(CH_SW + 4))
            tile_low(At(TI_SW + 1), k_lo[:, 1, :], k_hi[:, 1, :])
            v_low(At(UNITS_NA), slice(0, 4))
            dve.wait_ge(vt_done, UNITS_NA + 1)
            scale(At(CH_SW + 3), At(GR_SW + 3), vT[:, :], 1.0)
            split_weights(At(CH_SW + 5))
            queries(At(0))
            v_low(At(UNITS_NA + 1), slice(4, 8))
            sw_step(At(1), before=False)
            with dve.Fori(0, 3) as i:
                for n in range(2):
                    sw_step(At(2 + n, 2, i))
            sw_step(At(8), dense=False)
            sw_pt_low(At(7), 3)
            sw_o_low(At(7), 1)
            clear_squares(3)
            output_projection(CH_SWO, GR_SWO, 3)
            mlp(CH_MLP1, GR_MLP1, TI_MLP1, 3)
            reciprocal_deviation(4)
            for k in range(KT):
                nc.vector.scalar_tensor_tensor(out=x[:, k, :], in0=x[:, k, :],
                                               scalar=gain[:, 4 * KT + k:4 * KT + k + 1], in1=rstd[:],
                                               op0=ALU.mult, op1=ALU.mult).then_inc(y_made, 1)



def blocks_of(w):
    k, m = w.shape
    t = w.reshape(k // P, P, m // P, P).transpose(2, 0, 1, 3).reshape(-1, BLOCKS, P, P)
    return t.transpose(0, 2, 1, 3).reshape(-1, P, CHUNK)


def sw_heads():
    return [8 * (t % 2) + 4 * hh + t // 2 for t in range(PAIRS) for hh in range(2)]


def mask_constant():
    col = np.arange(COLS)
    start = np.clip(col - NA_COLS // 2, 0, COLS - NA_COLS)
    m = np.full((ROWS, QC, QT, WC), LOWEST, np.float32)
    for j in range(QT):
        for q in range(QC):
            key = WIN0[j] + np.arange(WC)
            s = start[QC * j + q]
            m[:, q, j, (key >= s) & (key < s + NA_COLS)] = 0.0
    return m.reshape(P, QT, WC)


def onehot_constant():
    buckets, exact, farthest = 32, 8, 128
    half = buckets // 2
    rel = np.arange(-P, P + 1)
    n = np.abs(rel)
    nf = np.maximum(n, 1).astype(np.float32)
    large = exact + (np.log(nf / np.float32(exact)) / np.float32(np.log(farthest / exact))
                     * np.float32(half - exact)).astype(np.int32)
    bucket = np.where(rel > 0, half, 0) + np.where(n < exact, n, np.minimum(large, half - 1))
    return (bucket[None, :] == np.arange(buckets)[:, None]).astype(np.float32)


def kernel(x, mix_norm, mlp_norm, final_norm, na_w_qkv, na_rpb, na_w_o, swa_w_qkv, swa_sinks, swa_w_o,
           t5_rel_table, mlp_w_in, mlp_w_out):
    import concourse.bacc as bacc
    from concourse.bass_utils import run_bass_kernel_spmd

    arr = np.asarray
    na, sw = arr(na_w_qkv)[0], arr(swa_w_qkv)[0]
    na_qkv = na.reshape(D, 3, KT, P).transpose(0, 2, 1, 3).reshape(D, 3 * D)
    heads = sw_heads()
    sw_q = sw[:, :D].reshape(D, HEADS, HD)[:, heads].reshape(D, D)
    sw_k, sw_v = sw[:, D:D + KV * HD], sw[:, D + KV * HD:]
    sw_kv = np.concatenate([sw_k[:, :P], sw_v[:, :P], sw_k[:, P:], sw_v[:, P:]], axis=1)
    sw_o = arr(swa_w_o)[0].reshape(HEADS, HD, D)[heads].reshape(D, D)
    w_in, w_out = arr(mlp_w_in), arr(mlp_w_out)

    def mlp_chunks(n):
        out = []
        for half in range(2):
            s = slice(FF // 2 * half, FF // 2 * (half + 1))
            out += [blocks_of(w_in[n][:, s]), blocks_of(w_out[n][s])]
        return out

    stream = np.concatenate([blocks_of(na_qkv), blocks_of(arr(na_w_o)[0]), *mlp_chunks(0), blocks_of(sw_kv),
                             blocks_of(sw_q), blocks_of(sw_o), *mlp_chunks(1)])
    mix, mlp = arr(mix_norm), arr(mlp_norm)
    gains = np.stack([mix[0], mlp[0], mix[1], mlp[1], arr(final_norm)])
    arrays = {
        "in_xT": arr(x)[0].T.reshape(KT, P, SEQ),
        "in_wstream": stream,
        "in_gains": gains.reshape(NORMS * KT, P).T,
        "in_rpb": arr(na_rpb)[0],
        "in_sinks": arr(swa_sinks)[0][heads],
        "in_rel_table": arr(t5_rel_table)[:, heads],
        "in_mask": mask_constant(),
        "in_onehot": onehot_constant(),
    }
    arrays = {k: np.ascontiguousarray(a) for k, a in arrays.items()}
    nc = bacc.Bacc("TRN2", target_bir_lowering=False, num_devices=1)
    args = [nc.dram_tensor(k, a.shape, mybir.dt.from_np(a.dtype), kind="ExternalInput").ap()
            for k, a in arrays.items()]
    out = nc.dram_tensor("out_y", (KT, P, SEQ), F32, kind="ExternalOutput").ap()
    encoder(nc, *args, out)
    r = run_bass_kernel_spmd(nc, [arrays], core_ids=[0])
    return np.ascontiguousarray(arr(r.results[0]["out_y"]).reshape(D, SEQ).T).reshape(1, SEQ, D)
```

```python
import numpy as np
from contextlib import ExitStack

import concourse.bass as bass
from concourse import mybir

F32 = mybir.dt.float32
F32R = mybir.dt.float32r
ALU = mybir.AluOpType
ACT = mybir.ActivationFunctionType

P = 128
D, SEQ, FF = 1024, 512, 4096
HD, HEADS, KV = 64, 16, 4
ROWS, COLS = 8, 64
NA_COLS = 16
KT = D // P
PAIRS = HEADS // 2
QT = SEQ // P
BLOCKS = 8
CHUNK = BLOCKS * P
HALF = FF // 2 // P
EPS = 1e-6
LOWEST = -3.0e38

QC = COLS // QT
WC = 32
WIN0 = [min(max(QC * j - NA_COLS // 2, 0), COLS - WC) for j in range(QT)]
U0 = [WIN0[j] - QC * j + NA_COLS for j in range(QT)]
BIASC = 48
RPB_R, RPB_C = 2 * ROWS - 1, 2 * NA_COLS - 1
PITCH = 64

SW_TILES = [[(0, 0, 2), (1, 0, 3)], [(3, 2, 2), (2, 1, 3)]]
BAND = 3 * P
RELS = 2 * P + 1
T5_W = P - QC + BAND
UNIT = 5 * P

CH_NA, CH_NAO, CH_MLP0 = 0, 24, 32
CH_SW, CH_SWO, CH_MLP1 = 96, 108, 116
CHUNKS = 180
GR_NA, GR_NAO, GR_MLP0, GR_SW, GR_SWO, GR_MLP1 = 0, 24, 32, 80, 92, 100
EARLY = 4
EARLY_BLOCKS = ([(g, k) for g in (0, 1) for k in range(4)]
                + [(g, k) for g in (0, 1) for k in (4, 5)] + [(0, 6), (1, 6), (2, 0), (3, 0)]
                + [(g, k) for k in range(1, 5) for g in (2, 3)]
                + [(g, k) for k in (5, 6) for g in (2, 3)] + [(g, 7) for g in range(EARLY)])
NA_EARLY = [(0, 8), (8, 14), (14, 20)]
SPLIT_AFTER = {0: 5, 2: 6, 5: 7, 6: 8, 7: 9}
UNITS_NA = 2 * PAIRS
TI_NA, TI_MLP0, TI_SW, TI_MLP1 = 0, 16, 48, 58
NORMS = 5


class At:

    def __init__(self, a, b=0, i=None):
        self.a, self.b, self.i = a, b, i

    def __add__(self, n):
        return At(self.a + n, self.b, self.i)

    def __mul__(self, n):
        return At(self.a * n, self.b * n, self.i)

    @property
    def v(self):
        return self.a if self.i is None or self.b == 0 else self.i * self.b + self.a

    @property
    def half(self):
        return At(self.a // 2, self.b // 2, self.i)

    @property
    def odd(self):
        return self.a % 2


def encoder(nc, xT, wstream, gains, rpb, sinks, rel_table, na_mask, onehot, out):
    t5_dram = nc.dram_tensor("t5_shifted", (QC, HEADS, T5_W), F32, kind="Internal").ap()
    rpb_dram = nc.dram_tensor("rpb_shifted", (QC, HEADS, RPB_R, BIASC), F32, kind="Internal").ap()

    with ExitStack() as ctx:
        def sb(name, shape, dt=F32):
            return ctx.enter_context(nc.sbuf_tensor(name, shape, dt))

        def sem(name):
            return ctx.enter_context(nc.semaphore(name))

        x = sb("x_res", [P, KT, SEQ])
        h_hi, h_lo = sb("h_hi", [P, KT, SEQ], F32R), sb("h_lo", [P, KT, SEQ], F32R)
        w_raw = sb("w_raw", [P, 2, CHUNK])
        w_hi, w_lo = sb("w_hi", [P, 2, CHUNK], F32R), sb("w_lo", [P, 2, CHUNK], F32R)
        u_hi, u_lo = sb("u_hi", [P, HALF, SEQ], F32R), sb("u_lo", [P, HALF, SEQ], F32R)
        k_hi, k_lo = sb("k_hi", [P, 2, SEQ], F32R), sb("k_lo", [P, 2, SEQ], F32R)
        v_hi, v_lo = sb("v_hi", [P, 8, P], F32R), sb("v_lo", [P, 8, P], F32R)
        pt_hi, pt_lo = sb("pt_hi", [P, 8, P], F32R), sb("pt_lo", [P, 8, P], F32R)
        bias = sb("bias_all", [P, HEADS, BAND])
        probs = sb("probs", [P, 2 * UNIT])
        vT = sb("vT", [P, SEQ])
        bias_m = sb("bias_masked", [P, QT, WC, ROWS])
        onehot_sb = sb("onehot_sb", [32, RELS])
        sqsum = sb("sqsum", [P, SEQ])
        rstd = sb("rstd", [P, SEQ])
        scaled = sb("scaled", [P, 2, SEQ])
        ident, ones = sb("ident", [P, P]), sb("ones", [P, P])
        mask = sb("mask", [P, QT, WC])
        gain = sb("gain", [P, NORMS * KT])
        eps, one = sb("eps", [P, 1]), sb("one", [P, 1])
        sink, nsink = sb("sink", [P, HEADS]), sb("nsink", [P, HEADS])
        table = sb("table", [32, HEADS])
        nmax, rsum = sb("nmax", [P, 2, QT]), sb("rsum", [P, 2, QT])
        esink, rden = sb("esink", [P, 2, QT]), sb("rden", [P, 2, QT])
        rpb_pad = bias[0:HEADS, 0:3, :].rearrange("p a b -> p (a b)")[:, 0:RPB_R * PITCH]
        rpb_pad = rpb_pad.rearrange("p (r c) -> p r c", c=PITCH)
        t5_row = vT[0:HEADS, :]
        sw_bias = bias_m.rearrange("p a b c -> p (a b c)").rearrange("p (h n) -> p h n", h=2)
        sw_sink, sw_nsink = sb("sw_sink", [P, 2]), sb("sw_nsink", [P, 2])

        acc = [ctx.enter_context(nc.psum_tensor(f"acc{n}", [P, SEQ], F32)) for n in range(2)]
        s_ps = ctx.enter_context(nc.psum_tensor("s_ps", [P, 2, 512], F32))
        pt_ps = ctx.enter_context(nc.psum_tensor("pt_ps", [P, 8, P], F32))
        o_ps = ctx.enter_context(nc.psum_tensor("o_ps", [HD, SEQ], F32))
        misc_ps = ctx.enter_context(nc.psum_tensor("misc_ps", [P, QT, P], F32))

        w_landed = [sem("w_landed0"), sem("w_landed1")]
        x_landed = [sem(f"x_landed{k}") for k in range(KT)]
        gain_landed, consts_landed, table_landed = sem("gain_landed"), sem("consts_landed"), sem("table_landed")
        rpb_landed, rpb_stored, t5_stored = sem("rpb_landed"), sem("rpb_stored"), sem("t5_stored")
        na_bias_landed, t5_bias_landed, y_stored = sem("na_bias_landed"), sem("t5_bias_landed"), sem("y_stored")
        filled, pool_filled, ident_made = sem("filled"), sem("pool_filled"), sem("ident_made")
        t5_product, t5_cleared, t5_made = sem("t5_product"), sem("t5_cleared"), sem("t5_made")
        nsink_made = sem("nsink_made")
        w_hi_made, w_split, w_used = sem("w_hi_made"), sem("w_split"), sem("w_used")
        acc_taken = sem("acc_taken")
        early_done = sem("early_done")
        squared, tile_hi, tile_split = sem("squared"), sem("tile_hi"), sem("tile_split")
        x_prepared, h_split, sq_cleared = sem("x_prepared"), sem("h_split"), sem("sq_cleared")
        stat_done, std_made, rstd_made = sem("stat_done"), sem("std_made"), sem("rstd_made")
        bias_made, logits_begun = sem("bias_made"), sem("logits_begun")
        scores_done, logits_made, probs_made = sem("scores_done"), sem("logits_made"), sem("probs_made")
        pt_done, pt_hi_made, pt_split, pv_done = sem("pt_done"), sem("pt_hi_made"), sem("pt_split"), sem("pv_done")
        probs_scaled = sem("probs_scaled")
        vt_done, v_hi_made, v_split = sem("vt_done"), sem("v_hi_made"), sem("v_split")
        den_made = sem("den_made")
        first_logits = sem("first_logits")
        o_hi_made, o_split = sem("o_hi_made"), sem("o_split")
        y_made = sem("y_made")

        def f32(ap):
            return ap.bitcast(F32)

        def tokens(t):
            return t.rearrange("p (r c) -> p r c", c=COLS)

        def by_column(t):
            return t.rearrange("p (c r) -> p r c", r=ROWS)

        def in_tiles(t):
            return t.rearrange("p (j r c) -> p j r c", j=QT, c=QC)

        def by_tile(t):
            return t.rearrange("p (r j c) -> p j r c", j=QT, c=QC)

        def window(j):
            return slice(WIN0[j] * ROWS, (WIN0[j] + WC) * ROWS)

        def flat(t):
            return t.rearrange("p a b -> p (a b)")

        na_probs = probs[:, 0:QT * ROWS * WC].rearrange("p (j n) -> p j n", j=QT)

        def sw_probs(n, tile, blocks):
            at = (n % 2) * UNIT + 2 * P * tile
            return probs[:, at:at + blocks * P]

        def sw_unit_by(p, n, by):
            return p + (n + by) // 4, (n + by) % 4

        def sw_unit(p, n):
            return p * 4 + (UNITS_NA + n)

        block = ctx.enter_context(nc.Block())

        @block.sync
        def _(sp):
            def load_weights(c):
                if c.a >= 2 or c.b:
                    sp.wait_ge(w_split, (c + -1).v)
                sp.dma_start(w_raw[:, c.odd, :], wstream[c.v]).then_inc(w_landed[c.odd], 16)

            load_weights(At(0))
            for k in range(2):
                sp.dma_start(x[:, k, :], xT[k]).then_inc(x_landed[k], 16)
            sp.wait_ge(pool_filled, 2)
            sp.dma_start(rpb_pad[:, :, NA_COLS:NA_COLS + RPB_C], rpb).then_inc(rpb_landed, 16)
            for k in range(2, KT):
                sp.dma_start(x[:, k, :], xT[k]).then_inc(x_landed[k], 16)
            load_weights(At(1))
            sp.wait_ge(rpb_landed, 16)
            for c in range(QC):
                sp.dma_start(rpb_dram[c], rpb_pad[:, :, QC - 1 - c:QC - 1 - c + BIASC]).then_inc(rpb_stored, 16)
            load_weights(At(2))
            load_weights(At(3))
            sp.wait_ge(rpb_stored, 16 * QC)
            for r in range(ROWS):
                sp.dma_start(bias[QC * r:QC * (r + 1), :, :],
                             rpb_dram[:, :, ROWS - 1 - r:RPB_R - r, :].rearrange("c h r u -> c h (r u)")
                             ).then_inc(na_bias_landed, 16)
            with sp.Fori(2, CHUNKS // 2) as i:
                for n in range(2):
                    load_weights(At(n, 2, i))
            for k in range(KT):
                sp.wait_ge(y_made, k + 1)
                sp.dma_start(out[k], x[:, k, :]).then_inc(y_stored, 16)
            sp.wait_ge(y_stored, 16 * KT)

        @block.gpsimd
        def _(pool):
            nc.gpsimd.memset(rpb_pad, 0.0).then_inc(pool_filled, 1)
            nc.gpsimd.memset(ident[:], 0.0).then_inc(pool_filled, 1)
            pool.wait_ge(pool_filled, 2)
            nc.gpsimd.affine_select(out=ident[:], in_=ident[:], compare_op=ALU.not_equal, fill=1.0, base=0,
                                    pattern=[[-1, P]], channel_multiplier=1).then_inc(ident_made, 1)
            pool.dma_start(mask[:], na_mask).then_inc(consts_landed, 16)
            pool.dma_start(table[:], rel_table).then_inc(table_landed, 16)
            pool.dma_start(onehot_sb[:], onehot).then_inc(table_landed, 16)
            pool.dma_start(sink[:], sinks.partition_broadcast(P)).then_inc(consts_landed, 16)
            pool.wait_ge(na_bias_landed, 16 * ROWS)
            pool.wait_ge(consts_landed, 16 * 2)

            def masked_bias(h):
                rows = bias[:, h.v, :].rearrange("p (r u) -> p r u", u=BIASC)
                for j in range(QT):
                    ins = nc.gpsimd.tensor_tensor(bias_m[:, j, :, :].rearrange("p c r -> p r c"),
                                                  rows[:, :, U0[j]:U0[j] + WC],
                                                  mask[:, j:j + 1, :].to_broadcast([P, ROWS, WC]), ALU.add)
                ins.then_inc(bias_made, 1)

            masked_bias(At(0))
            with pool.Fori(1, HEADS) as i:
                pool.wait_ge(logits_made, i)
                masked_bias(At(0, 1, i))
            pool.wait_ge(bias_made, HEADS)
            pool.wait_ge(t5_made, 1)
            for q in range(QC):
                pool.dma_start(t5_dram[q], t5_row[:, QC - 1 - q:QC - 1 - q + T5_W]).then_inc(t5_stored, 16)
            pool.wait_ge(t5_stored, 16 * QC)
            for a in range(P // QC):
                at = P - QC - QC * a
                pool.dma_start(bias[QC * a:QC * (a + 1), :, :], t5_dram[:, :, at:at + BAND]
                               ).then_inc(t5_bias_landed, 16)

            pool.wait_ge(nsink_made, 1)
            pool.wait_ge(t5_bias_landed, 16 * P // QC)

            def head_bias(pair, hh):
                head = pair * 2 + hh
                nc.gpsimd.tensor_copy(sw_bias[:, hh, 0:BAND], bias[:, head.v, :])
                nc.gpsimd.tensor_copy(sw_sink[:, hh:hh + 1], sink[:, bass.ds(head.v, 1)])
                nc.gpsimd.tensor_copy(sw_nsink[:, hh:hh + 1], nsink[:, bass.ds(head.v, 1)]).then_inc(bias_made, 1)

            pool.wait_ge(logits_made, UNITS_NA)
            head_bias(At(0), 0)
            head_bias(At(0), 1)
            with pool.Fori(1, PAIRS) as i:
                for hh in range(2):
                    pair = At(0, 1, i)
                    pool.wait_ge(probs_made, sw_unit(pair, 2 * hh - 2).v)
                    head_bias(pair, hh)

        @block.tensor
        def _(pe):
            def product(dst, a, b, start, stop):
                nc.tensor.matmul(dst, a[0], b[0], start=start, stop=False)
                nc.tensor.matmul(dst, a[0], b[1], start=False, stop=False)
                return nc.tensor.matmul(dst, a[1], b[0], start=False, stop=stop)

            def h_tile(k):
                return h_hi[:, k, :], h_lo[:, k, :]

            def u_tile(k):
                return u_hi[:, k, :], u_lo[:, k, :]

            def part(c, g, tile, ks, k0=0, first=True, last=True, taken=False):
                if ks[0] == 0:
                    pe.wait_ge(w_split, (c + 1).v)
                    if first and g.a >= 2 and not taken:
                        pe.wait_ge(acc_taken, (g + -1).v)
                for k in ks:
                    b = slice(k * P, (k + 1) * P)
                    ins = product(acc[g.odd][:], (w_hi[:, c.odd, b], w_lo[:, c.odd, b]), tile(k0 + k),
                                  first and k == 0, last and k == BLOCKS - 1)
                if ks[-1] == BLOCKS - 1:
                    ins.then_inc(w_used, 1)

            ALL = range(BLOCKS)

            def early_part(ch, gr, heads_before, start, stop):
                heads = 0
                for n in range(start, stop):
                    (g, k), c, b = EARLY_BLOCKS[n], n // BLOCKS, slice(n % BLOCKS * P, (n % BLOCKS + 1) * P)
                    if n % BLOCKS == 0:
                        pe.wait_ge(w_split, ch + c + 1)
                    if k == 0 and g < 2:
                        pe.wait_ge(acc_taken, gr + g - 1)
                    if k == 0 and g == 2:
                        pe.wait_ge(logits_made, UNITS_NA + (4 * PAIRS if heads_before else 0))
                    if 2 * (k + 1) > heads:
                        heads = 2 * (k + 1)
                        pe.wait_ge(o_split, heads_before + heads)
                    bank = acc[g][:] if g < 2 else s_ps[:, g - 2, :]
                    odd = (ch + c) % 2
                    ins = product(bank, (w_hi[:, odd, b], w_lo[:, odd, b]), u_tile(k), k == 0, k == KT - 1)
                    if n % BLOCKS == BLOCKS - 1:
                        ins.then_inc(w_used, 1)
                    elif k == KT - 1:
                        ins.then_inc(early_done, 1)

            def statistics(n):
                pe.wait_ge(h_split, KT * (n + 1))
                nc.tensor.matmul(flat(misc_ps[:]), ones[:], sqsum[:], start=True, stop=True).then_inc(stat_done, 1)

            def part_after_norm(c, g, n):
                for k in ALL:
                    pe.wait_ge(h_split, KT * n + k + 1)
                    if k == KT - 1:
                        statistics(n)
                    part(c, g, h_tile, [k])

            def transpose_v(blocks):
                for n, src in enumerate(blocks):
                    ins = nc.tensor.transpose(misc_ps[:, n, :], src, ident[:])
                ins.then_inc(vt_done, 1)

            def na_scores(p, hh):
                unit = p * 2 + hh
                if unit.a >= 1:
                    pe.wait_ge(logits_made, unit.v)
                s, q = slice(HD * hh, HD * (hh + 1)), 8 + p.odd
                for j in range(QT):
                    qs, ks = slice(P * j, P * (j + 1)), window(j)
                    ins = product(s_ps[:, j // 2, 256 * (j % 2):256 * (j % 2 + 1)],
                                  (u_hi[s, q, qs], u_lo[s, q, qs]),
                                  (k_hi[s, p.odd, ks], k_lo[s, p.odd, ks]), True, True)
                ins.then_inc(scores_done, 1)

            def na_transpose(p, hh):
                unit = p * 2 + hh
                pe.wait_ge(probs_scaled, (unit + 1).v)
                if unit.a >= 1:
                    pe.wait_ge(pt_split, unit.v)
                for j in range(QT):
                    for b in range(2):
                        ins = nc.tensor.transpose(pt_ps[:, 2 * j + b, :], na_probs[:, j, b * P:(b + 1) * P],
                                                  ident[:])
                ins.then_inc(pt_done, 1)

            def na_values(p, hh):
                head = p * 2 + hh
                pe.wait_ge(pt_split, (head + 1).v)
                pe.wait_ge(v_split, (p * 2 + 2).v)
                if head.a >= 1:
                    pe.wait_ge(o_split, head.v)
                s = slice(HD * hh, HD * (hh + 1))
                for j in range(QT):
                    for b in range(2):
                        n = 2 * j + b
                        ins = product(o_ps[:, P * j:P * (j + 1)], (v_hi[:, n, s], v_lo[:, n, s]),
                                      (pt_hi[:, n, :], pt_lo[:, n, :]), b == 0, b == 1)
                ins.then_inc(pv_done, 1)

            def na_v_blocks(p, batch):
                if batch == 0:
                    pe.wait_ge(acc_taken, (p * 3 + (GR_NA + 3)).v)
                    if p.a >= 1:
                        pe.wait_ge(v_split, (p * 2).v)
                else:
                    pe.wait_ge(v_split, (p * 2 + 1).v)
                transpose_v([vT[:, window(2 * batch + j)][:, P * b:P * (b + 1)] for j in range(2) for b in range(2)])

            def na_step(m, dense=True, attend=True):
                p, c, g = m + -1, m * 3 + CH_NA, m * 3 + GR_NA

                def dense_part(n):
                    if dense and m.a == 0 and n == 0:
                        part_after_norm(c, g, 0)
                    elif dense:
                        part(c + n, g + n, h_tile, ALL)
                    else:
                        early_part(CH_NAO, GR_NAO, 0, *NA_EARLY[n])

                if attend:
                    pe.wait_ge(tile_split, (p * 2 + (TI_NA + 2)).v)
                    na_scores(p, 0)
                    na_v_blocks(p, 0)
                dense_part(0)
                if attend:
                    na_transpose(p, 0)
                    na_v_blocks(p, 1)
                    na_scores(p, 1)
                dense_part(1)
                if attend:
                    na_values(p, 0)
                    na_transpose(p, 1)
                dense_part(2)
                if attend:
                    na_values(p, 1)

            def output_projection(ch, gr, heads_before, start):
                early_part(ch, gr, heads_before, start, len(EARLY_BLOCKS))
                for n in range(2):
                    pe.wait_ge(acc_taken, gr + n + 1)
                    part(At(ch + EARLY + n), At(gr + EARLY + n), u_tile, ALL, taken=True)
                for n in range(2, 4):
                    part(At(ch + EARLY + n), At(gr + EARLY + n), u_tile, ALL)

            def mlp(ch, gr, ti, norm):
                for half in range(2):
                    c0, g0 = ch + 32 * half, gr + 24 * half
                    start = 0
                    if half == 0:
                        part_after_norm(At(c0), At(g0), norm)
                        part(At(c0 + 1), At(g0 + 1), h_tile, ALL)
                        start = 1
                    with pe.Fori(start, HALF // 2) as i:
                        for n in range(2):
                            part(At(c0 + n, 2, i), At(g0 + n, 2, i), h_tile, ALL)
                    split = ti + HALF * half
                    with pe.Fori(0, KT // 2) as i:
                        for n in range(2):
                            c, g = At(c0 + HALF + 2 * n, 4, i), At(g0 + HALF + n, 2, i)
                            pe.wait_ge(tile_split, split + BLOCKS)
                            part(c, g, u_tile, ALL, 0, True, False)
                            pe.wait_ge(tile_split, split + HALF - 2)
                            part(c + 1, g, u_tile, range(6), BLOCKS, False, True)
                            pe.wait_ge(tile_split, split + HALF)
                            part(c + 1, g, u_tile, range(6, BLOCKS), BLOCKS, False, True)

            def sw_scores(p, n):
                hh = n // 2
                if n == 0:
                    pe.wait_ge(tile_split, (p + (TI_SW + 3)).v)
                pe.wait_ge(logits_made, sw_unit(p, n).v)
                s, q, kv = slice(HD * hh, HD * (hh + 1)), 8 + p.odd, p.odd
                for tile, (i, kb, nb) in enumerate(SW_TILES[n % 2]):
                    qs, ks = slice(P * i, P * (i + 1)), slice(P * kb, P * (kb + nb))
                    ins = product(s_ps[:, tile, 0:nb * P], (u_hi[s, q, qs], u_lo[s, q, qs]),
                                  (k_hi[s, kv, ks], k_lo[s, kv, ks]), True, True)
                ins.then_inc(scores_done, 1)

            def sw_transpose(p, n):
                unit = sw_unit(p, n)
                pe.wait_ge(probs_scaled, (unit + 1).v)
                pe.wait_ge(pt_split, unit.v)
                at = 0
                for tile, (i, kb, nb) in enumerate(SW_TILES[n % 2]):
                    for b in range(nb):
                        ins = nc.tensor.transpose(pt_ps[:, at, :], sw_probs(n, tile, nb)[:, b * P:(b + 1) * P],
                                                  ident[:])
                        at += 1
                ins.then_inc(pt_done, 1)

            def sw_values(p, n):
                hh, kv, at = n // 2, p.odd, 0
                pe.wait_ge(pt_split, (sw_unit(p, n) + 1).v)
                if n % 2 == 0:
                    pe.wait_ge(o_split, (p * 2 + (HEADS + hh)).v)
                s = slice(HD * hh, HD * (hh + 1))
                for i, kb, nb in SW_TILES[n % 2]:
                    for b in range(nb):
                        v = 4 * kv + kb + b
                        ins = product(o_ps[:, P * i:P * (i + 1)], (v_hi[:, v, s], v_lo[:, v, s]),
                                      (pt_hi[:, at, :], pt_lo[:, at, :]), b == 0, b == nb - 1)
                        at += 1
                ins.then_inc(pv_done, 1)

            def sw_v_blocks(kv):
                pe.wait_ge(acc_taken, GR_SW + 2 * kv + 2)
                if kv:
                    pe.wait_ge(v_split, UNITS_NA + 1)
                transpose_v([vT[:, b * P:(b + 1) * P] for b in range(QT)])

            def sw_step(m, before=True, last=None):
                p, c, g = m + -1, m + (CH_SW + 4), m + (GR_SW + 4)

                def dense_part(n):
                    if last == 8:
                        early_part(CH_SWO, GR_SWO, HEADS, n + 4, n + 5)
                    elif n < 4:
                        part(c, g, h_tile, [4 + n])
                    elif last == 7:
                        early_part(CH_SWO, GR_SWO, HEADS, n - 4, n - 3)
                    else:
                        part(c + 1, g + 1, h_tile, [n - 4])

                for n in range(4):
                    if before or n >= 1:
                        sw_transpose(*sw_unit_by(p, n, -1))
                    dense_part(2 * n)
                    if n < 3 or last != 8:
                        sw_scores(*sw_unit_by(p, n, 1))
                    dense_part(2 * n + 1)
                    if before or n >= 1:
                        sw_values(*sw_unit_by(p, n, -1))

            pe.wait_ge(filled, 1)
            pe.wait_ge(ident_made, 1)
            na_step(At(0), attend=False)
            na_step(At(1))
            with pe.Fori(0, 3) as i:
                for n in range(2):
                    na_step(At(2 + n, 2, i))
            na_step(At(8), dense=False)
            pe.wait_ge(table_landed, 16 * 2)
            nc.tensor.matmul(flat(misc_ps[:])[0:HEADS, 0:RELS], table[:], onehot_sb[:], start=True,
                             stop=True).then_inc(t5_product, 1)
            output_projection(CH_NAO, GR_NAO, 0, NA_EARLY[-1][1])
            mlp(CH_MLP0, GR_MLP0, TI_MLP0, 1)
            part_after_norm(At(CH_SW), At(GR_SW), 2)
            part(At(CH_SW + 1), At(GR_SW + 1), h_tile, ALL)
            part(At(CH_SW + 2), At(GR_SW + 2), h_tile, ALL)
            sw_v_blocks(0)
            part(At(CH_SW + 3), At(GR_SW + 3), h_tile, ALL)
            part(At(CH_SW + 4), At(GR_SW + 4), h_tile, ALL)
            sw_v_blocks(1)
            part(At(CH_SW + 5), At(GR_SW + 5), h_tile, range(4))
            pe.wait_ge(v_split, UNITS_NA + 2)
            sw_scores(At(0), 0)
            sw_step(At(1), before=False)
            with pe.Fori(0, 2) as i:
                for n in range(2):
                    sw_step(At(2 + n, 2, i))
            sw_step(At(6))
            sw_step(At(7), last=7)
            sw_step(At(8), last=8)
            sw_transpose(At(7), 3)
            early_part(CH_SWO, GR_SWO, HEADS, 12, 16)
            sw_values(At(7), 3)
            output_projection(CH_SWO, GR_SWO, HEADS, 2 * BLOCKS)
            mlp(CH_MLP1, GR_MLP1, TI_MLP1, 3)
            statistics(4)

        @block.scalar
        def _(act):
            def split_weights(c):
                if c.a >= 2:
                    act.wait_ge(w_used, (c + -1).v)
                act.wait_ge(w_landed[c.odd], ((c.half + 1) * 16).v)
                nc.scalar.copy(w_hi[:, c.odd, :], w_raw[:, c.odd, :]).then_inc(w_hi_made, 1)

            def prepare_x(n, k, landed):
                tile = k + KT * n
                landed()
                if tile.a >= 2:
                    act.wait_ge(h_split, (tile + -1).v)
                act.wait_ge(gain_landed, 16)
                if n < NORMS - 1:
                    nc.scalar.activation(h_hi[:, k.v, :], x[:, k.v, :], ACT.Copy, scale=gain_of(n, k))
                nc.scalar.activation(probs[:, SEQ * k.odd:SEQ * (k.odd + 1)], x[:, k.v, :],
                                     ACT.Square).then_inc(x_prepared, 1)

            def gain_of(n, k):
                at = k + KT * n
                return gain[:, bass.ds(at.v, 1)]

            def load_sqrt():
                nc.scalar.activation(one[:, 0:1], ones[:, 0:1], ACT.Sqrt)

            def deviation(n):
                act.wait_ge(stat_done, n + 1)
                nc.scalar.activation(rstd[:], flat(misc_ps[:]), ACT.Sqrt, bias=eps[:], scale=1.0 / D
                                     ).then_inc(std_made, 1)

            def tile_high(g, e, dst, square=None, order=None):
                act.wait_ge(acc_taken, (g + 1).v)
                src = scaled[:, e.odd, :]
                if square is not None:
                    nc.scalar.activation(src, src, ACT.Square).then_inc(squared, 1)
                    act.wait_ge(squared, (square + 1).v)
                if order is not None:
                    dst, src = order[0](dst), order[1](src)
                nc.scalar.copy(dst, src).then_inc(tile_hi, 1)

            def v_high(batch, dst):
                act.wait_ge(vt_done, (batch + 1).v)
                nc.scalar.copy(dst, misc_ps[:]).then_inc(v_hi_made, 1)

            def exponent(src, slot, i):
                return nc.scalar.activation(src, src, ACT.Exp, bias=nmax[:, slot, i:i + 1], scale=-1.0,
                                            accum_out=rsum[:, slot, i:i + 1])

            def pt_high(unit, blocks):
                act.wait_ge(pt_done, (unit + 1).v)
                nc.scalar.copy(pt_hi[:, 0:blocks, :], pt_ps[:, 0:blocks, :]).then_inc(pt_hi_made, 1)

            def o_high(unit, head, tile, hh, grid):
                act.wait_ge(pv_done, (unit + 1).v)
                dst, src = u_hi[HD * hh:HD * (hh + 1), tile.v, :], o_ps[:, :]
                if grid:
                    dst, src = by_tile(dst), in_tiles(src)
                nc.scalar.copy(dst, src).then_inc(o_hi_made, 1)

            def na_exp(p, hh):
                unit = p * 2 + hh
                act.wait_ge(logits_made, (unit + 1).v)
                for j in range(QT):
                    ins = exponent(na_probs[:, j, :], hh, j)
                ins.then_inc(probs_made, 1)

            def na_step(m, dense=True, attend=True):
                p, c, g = m + -1, m * 3 + CH_NA, m * 3 + GR_NA
                if attend:
                    v_high(p * 2, v_hi[:, 0:4, :])
                    na_exp(p, 0)
                if dense:
                    if m.a == 0:
                        load_sqrt()
                        deviation(0)
                    split_weights(c + 2)
                    tile_high(g, m * 2 + TI_NA, u_hi[:, 8 + m.odd, :], order=(in_tiles, by_tile))
                if attend:
                    pt_high(p * 2, 8)
                    v_high(p * 2 + 1, v_hi[:, 4:8, :])
                    na_exp(p, 1)
                if dense:
                    split_weights(c + 3)
                    tile_high(g + 1, m * 2 + (TI_NA + 1), k_hi[:, m.odd, :], order=(by_column, tokens))
                if attend:
                    if not dense:
                        split_weights(At(CH_NAO + 2))
                    pt_high(p * 2 + 1, 8)
                    o_high(p * 2, p * 2, p, 0, True)
                split_weights(c + 4 if dense else At(CH_NAO + 3))
                if attend:
                    o_high(p * 2 + 1, p * 2 + 1, p, 1, True)

            def output_projection(ch, gr, norm):
                split_weights(At(ch + EARLY))
                for k in range(KT):
                    prepare_x(norm, At(k), lambda: act.wait_ge(acc_taken, gr + k + 1))
                    if k in SPLIT_AFTER:
                        split_weights(At(ch + SPLIT_AFTER[k]))
                load_sqrt()

            def mlp(ch, gr, ti, sq, norm):
                for half in range(2):
                    c0, g0 = ch + 32 * half, gr + 24 * half
                    if half == 0:
                        deviation(norm)
                    split_weights(At(c0 + 2))

                    def hidden(n, i, first=False):
                        f = At(n, 2, i) if i is not None else At(n)
                        if not first:
                            split_weights(f + (c0 + 2))
                        tile_high(f + g0, f + (ti + HALF * half), u_hi[:, f.v, :], f + (sq + HALF * half))

                    hidden(0, None, True)
                    hidden(1, None)
                    with act.Fori(1, HALF // 2) as i:
                        hidden(0, i)
                        hidden(1, i)

                    def down(n, i):
                        m = At(n, 2, i) if i is not None else At(n)
                        g = m + (g0 + HALF)
                        c = m * 2 + (c0 + HALF + 2)
                        if c.a < CHUNKS:
                            split_weights(c)
                        if half == 1:
                            prepare_x(norm + 1, m, lambda: act.wait_ge(acc_taken, (g + 1).v))
                        if (c + 1).a < CHUNKS:
                            split_weights(c + 1)

                    with act.Fori(0, KT // 2 - 1) as i:
                        down(0, i)
                        down(1, i)
                    down(KT - 2, None)
                    down(KT - 1, None)
                load_sqrt()

            def sw_exp(p, n, tile):
                i, kb, nb = SW_TILES[n % 2][tile]
                if tile == 0:
                    act.wait_ge(first_logits, (p * 4 + (n + 1)).v)
                else:
                    act.wait_ge(logits_made, (sw_unit(p, n) + 1).v)
                exponent(sw_probs(n, tile, nb), n % 2, tile)
                if tile == 1:
                    hh = n // 2
                    nc.scalar.activation(esink[:, n % 2, 0:2], nmax[:, n % 2, 0:2], ACT.Exp,
                                         bias=sw_sink[:, hh:hh + 1]).then_inc(probs_made, 1)

            def sw_pt_high(p, n):
                pt_high(sw_unit(p, n), UNIT // P)

            def sw_o_high(p, hh):
                o_high(sw_unit(p, 2 * hh + 1), p * 2 + (HEADS + hh), p, hh, False)

            def sw_step(m, before=True, dense=True):
                p = m + -1
                for n in range(4):
                    sw_exp(p, n, 0)
                    if before or n >= 1:
                        sw_pt_high(*sw_unit_by(p, n, -1))
                    sw_exp(p, n, 1)
                    if n == 0 and before:
                        sw_o_high(p + -1, 1)
                    if n == 2 and dense:
                        tile_high(m + (GR_SW + 4), m + (TI_SW + 2), u_hi[:, 8 + m.odd, :])
                    if n == 2:
                        sw_o_high(p, 0)
                    if n == 3:
                        split_weights(m + (CH_SW + 6))

            act.dma_start(gain[:], gains).then_inc(gain_landed, 16)
            act.wait_ge(filled, 2)
            nc.scalar.activation(one[:, 0:1], ones[:, 0:1], ACT.Square)
            split_weights(At(0))
            for k in range(KT):
                prepare_x(0, At(k), lambda: act.wait_ge(x_landed[k], 16))
                if k == 5:
                    split_weights(At(1))
            na_step(At(0), attend=False)
            na_step(At(1))
            with act.Fori(0, 3) as i:
                for n in range(2):
                    na_step(At(2 + n, 2, i))
            na_step(At(8), dense=False)
            output_projection(CH_NAO, GR_NAO, 1)
            mlp(CH_MLP0, GR_MLP0, TI_MLP0, 0, 1)
            deviation(2)
            split_weights(At(CH_SW + 2))
            tile_high(At(GR_SW), At(TI_SW), k_hi[:, 0, :])
            split_weights(At(CH_SW + 3))
            split_weights(At(CH_SW + 4))
            tile_high(At(GR_SW + 2), At(TI_SW + 1), k_hi[:, 1, :])
            v_high(At(UNITS_NA), v_hi[:, 0:4, :])
            split_weights(At(CH_SW + 5))
            split_weights(At(CH_SW + 6))
            tile_high(At(GR_SW + 4), At(TI_SW + 2), u_hi[:, 8, :])
            v_high(At(UNITS_NA + 1), v_hi[:, 4:8, :])
            sw_step(At(1), before=False)
            with act.Fori(0, 3) as i:
                for n in range(2):
                    sw_step(At(2 + n, 2, i))
            sw_step(At(8), dense=False)
            sw_pt_high(At(7), 3)
            split_weights(At(CH_SWO + 3))
            sw_o_high(At(7), 1)
            output_projection(CH_SWO, GR_SWO, 3)
            mlp(CH_MLP1, GR_MLP1, TI_MLP1, 32, 3)
            deviation(4)

        @block.vector
        def _(dve):
            def split_weights(c):
                dve.wait_ge(w_hi_made, (c + 1).v)
                nc.vector.tensor_tensor(w_lo[:, c.odd, :], w_raw[:, c.odd, :], f32(w_hi[:, c.odd, :]),
                                        ALU.subtract).then_inc(w_split, 1)

            def clear_squares(n):
                nc.vector.memset(sqsum[:], 0.0).then_inc(sq_cleared, 1)

            def finish_x(n, k):
                tile = k + KT * n
                dve.wait_ge(x_prepared, (tile + 1).v)
                if n < NORMS - 1:
                    nc.vector.scalar_tensor_tensor(out=h_lo[:, k.v, :], in0=x[:, k.v, :],
                                                   scalar=gain[:, bass.ds(tile.v, 1)], in1=f32(h_hi[:, k.v, :]),
                                                   op0=ALU.mult, op1=ALU.subtract)
                dve.wait_ge(sq_cleared, n + 1)
                if tile.a >= 1:
                    dve.wait_ge(h_split, tile.v)
                nc.vector.tensor_tensor(sqsum[:], sqsum[:], probs[:, SEQ * k.odd:SEQ * (k.odd + 1)],
                                        ALU.add).then_inc(h_split, 1)

            def reciprocal_deviation(n):
                dve.wait_ge(std_made, n + 1)
                nc.vector.reciprocal(rstd[:], rstd[:]).then_inc(rstd_made, 1)
                dve.wait_ge(rstd_made, n + 1)

            def scale(c, g, dst, factor, op=ALU.mult, order=lambda t: t):
                dve.wait_ge(w_used, (c + 1).v)
                nc.vector.scalar_tensor_tensor(out=dst, in0=order(acc[g.odd][:]), scalar=factor,
                                               in1=order(rstd[:]), op0=op, op1=ALU.mult).then_inc(acc_taken, 1)

            def scale_tile(c, g, e, factor, op=ALU.mult):
                if e.a >= 2:
                    dve.wait_ge(tile_split, (e + -1).v)
                scale(c, g, scaled[:, e.odd, :], factor, op)

            def tile_low(e, dst, hi, order=(lambda t: t, lambda t: t)):
                dve.wait_ge(tile_hi, (e + 1).v)
                nc.vector.tensor_tensor(order[0](dst), order[1](scaled[:, e.odd, :]), order[0](f32(hi)),
                                        ALU.subtract).then_inc(tile_split, 1)

            def v_low(batch, s):
                dve.wait_ge(v_hi_made, (batch + 1).v)
                nc.vector.tensor_tensor(v_lo[:, s, :], misc_ps[:], f32(v_hi[:, s, :]),
                                        ALU.subtract).then_inc(v_split, 1)

            def pt_low(unit, blocks):
                dve.wait_ge(pt_hi_made, (unit + 1).v)
                nc.vector.tensor_tensor(pt_lo[:, 0:blocks, :], pt_ps[:, 0:blocks, :], f32(pt_hi[:, 0:blocks, :]),
                                        ALU.subtract).then_inc(pt_split, 1)

            def o_low(head, tile, hh, grid):
                dve.wait_ge(o_hi_made, (head + 1).v)
                s = slice(HD * hh, HD * (hh + 1))
                hi, lo, src = f32(u_hi[s, tile.v, :]), u_lo[s, tile.v, :], o_ps[:, :]
                if grid:
                    hi, lo, src = by_tile(hi), by_tile(lo), in_tiles(src)
                nc.vector.tensor_tensor(lo, src, hi, ALU.subtract).then_inc(o_split, 1)

            def logits(dst, scores, add, start, slot, i):
                return nc.vector.tensor_tensor_reduce(out=dst, in0=scores, in1=add, scale=-1.0, scalar=start,
                                                      op0=ALU.add, op1=ALU.min, accum_out=nmax[:, slot, i:i + 1])

            def na_logits(p, hh):
                unit = p * 2 + hh
                dve.wait_ge(scores_done, (unit + 1).v)
                dve.wait_ge(bias_made, (unit + 1).v)
                if unit.a >= 1:
                    dve.wait_ge(pt_done, unit.v)
                dve.sem_inc(logits_begun, 1)
                for j in range(QT):
                    ins = logits(na_probs[:, j, :], s_ps[:, j // 2, 256 * (j % 2):256 * (j % 2 + 1)],
                                 bias_m[:, j, :, :].rearrange("p c r -> p (c r)"), -LOWEST, hh, j)
                ins.then_inc(logits_made, 1)

            def na_scale_probs(p, hh):
                unit = p * 2 + hh
                dve.wait_ge(probs_made, (unit + 1).v)
                nc.vector.reciprocal(rden[:, hh, :], rsum[:, hh, :]).then_inc(den_made, 1)
                dve.wait_ge(den_made, (unit + 1).v)
                for j in range(QT):
                    ins = nc.vector.tensor_scalar(na_probs[:, j, :], na_probs[:, j, :], rden[:, hh, j:j + 1], None,
                                                  ALU.mult)
                ins.then_inc(probs_scaled, 1)

            def na_step(m, dense=True, attend=True):
                p, c, g = m + -1, m * 3 + CH_NA, m * 3 + GR_NA
                if attend:
                    na_logits(p, 0)
                    v_low(p * 2, slice(0, 4))
                    na_scale_probs(p, 0)
                if dense:
                    if m.a == 0:
                        reciprocal_deviation(0)
                    e = m * 2 + TI_NA
                    scale_tile(c, g, e, HD ** -0.5)
                    split_weights(c + 2)
                    tile_low(e, u_lo[:, 8 + m.odd, :], u_hi[:, 8 + m.odd, :], (in_tiles, by_tile))
                if attend:
                    pt_low(p * 2, 8)
                    v_low(p * 2 + 1, slice(4, 8))
                    na_logits(p, 1)
                    na_scale_probs(p, 1)
                if dense:
                    e = m * 2 + (TI_NA + 1)
                    scale_tile(c + 1, g + 1, e, 1.0)
                    split_weights(c + 3)
                    tile_low(e, k_lo[:, m.odd, :], k_hi[:, m.odd, :], (by_column, tokens))
                if attend:
                    if not dense:
                        split_weights(At(CH_NAO + 2))
                    pt_low(p * 2 + 1, 8)
                    o_low(p * 2, p, 0, True)
                if dense:
                    scale(c + 2, g + 2, by_column(vT[:, :]), 1.0, order=tokens)
                split_weights(c + 4 if dense else At(CH_NAO + 3))
                if attend:
                    o_low(p * 2 + 1, p, 1, True)

            def add_to_x(c, g, k):
                dve.wait_ge(w_used, (c + 1).v)
                nc.vector.tensor_tensor(x[:, k.v, :], acc[g.odd][:], x[:, k.v, :], ALU.add).then_inc(acc_taken, 1)

            def add_early(ch, done_before, k):
                if k < EARLY - 1:
                    dve.wait_ge(early_done, done_before + k + 1)
                else:
                    dve.wait_ge(w_used, ch + EARLY)
                bank = acc[k][:] if k < 2 else s_ps[:, k - 2, :]
                nc.vector.tensor_tensor(x[:, k, :], bank, x[:, k, :], ALU.add).then_inc(acc_taken, 1)

            def output_projection(ch, gr, norm):
                def add(k):
                    if k < EARLY:
                        add_early(ch, 0 if norm == 1 else EARLY - 1, k)
                    else:
                        add_to_x(At(ch + k), At(gr + k), At(k))

                split_weights(At(ch + EARLY))
                add(0)
                for k in range(KT):
                    if k < EARLY - 1:
                        add(k + 1)
                    elif k >= EARLY:
                        add(k)
                    finish_x(norm, At(k))
                    if k in SPLIT_AFTER:
                        split_weights(At(ch + SPLIT_AFTER[k]))

            def mlp(ch, gr, ti, norm):
                for half in range(2):
                    c0, g0 = ch + 32 * half, gr + 24 * half
                    if half == 0:
                        reciprocal_deviation(norm)
                    with dve.Fori(0, HALF // 2) as i:
                        for n in range(2):
                            f = At(n, 2, i)
                            e = f + (ti + HALF * half)
                            scale_tile(f + c0, f + g0, e, 0.0, ALU.max)
                            split_weights(f + (c0 + 2))
                            tile_low(e, u_lo[:, f.v, :], u_hi[:, f.v, :])
                    if half == 1:
                        clear_squares(norm + 1)

                    def down(n, i):
                        m = At(n, 2, i) if i is not None else At(n)
                        c = m * 2 + (c0 + HALF)
                        if (c + 2).a < CHUNKS:
                            split_weights(c + 2)
                        add_to_x(c + 1, m + (g0 + HALF), m)
                        if half == 1:
                            finish_x(norm + 1, m)
                        if (c + 3).a < CHUNKS:
                            split_weights(c + 3)

                    with dve.Fori(0, KT // 2 - 1) as i:
                        down(0, i)
                        down(1, i)
                    down(KT - 2, None)
                    down(KT - 1, None)

            def sw_logits(p, n):
                unit, hh = sw_unit(p, n), n // 2
                head = p * 2 + hh
                dve.wait_ge(scores_done, (unit + 1).v)
                dve.wait_ge(bias_made, (head + (HEADS + 1)).v)
                dve.wait_ge(pt_done, (unit + -1).v)
                dve.sem_inc(logits_begun, 1)
                for tile, (i, kb, nb) in enumerate(SW_TILES[n % 2]):
                    at = (kb - i + 1) * P
                    ins = logits(sw_probs(n, tile, nb), s_ps[:, tile, 0:nb * P], sw_bias[:, hh, at:at + nb * P],
                                 sw_nsink[:, hh:hh + 1], n % 2, tile)
                    if tile == 0:
                        ins.then_inc(first_logits, 1)
                ins.then_inc(logits_made, 1)

            def sw_scale_probs(p, n):
                unit, slot = sw_unit(p, n), n % 2
                dve.wait_ge(probs_made, (unit + 1).v)
                nc.vector.tensor_tensor(rden[:, slot, 0:2], rsum[:, slot, 0:2], esink[:, slot, 0:2],
                                        ALU.add).then_inc(den_made, 1)
                dens = p * 8 + (UNITS_NA + 2 * n)
                dve.wait_ge(den_made, (dens + 1).v)
                nc.vector.reciprocal(rden[:, slot, 0:2], rden[:, slot, 0:2]).then_inc(den_made, 1)
                dve.wait_ge(den_made, (dens + 2).v)
                for tile, (i, kb, nb) in enumerate(SW_TILES[n % 2]):
                    t = sw_probs(n, tile, nb)
                    ins = nc.vector.tensor_scalar(t, t, rden[:, slot, tile:tile + 1], None, ALU.mult)
                ins.then_inc(probs_scaled, 1)

            def sw_pt_low(p, n):
                pt_low(sw_unit(p, n), UNIT // P)

            def sw_o_low(p, hh):
                o_low(p * 2 + (HEADS + hh), p, hh, False)

            def scale_queries(m):
                scale_tile(m + (CH_SW + 4), m + (GR_SW + 4), m + (TI_SW + 2), HD ** -0.5)

            def queries_low(m):
                tile_low(m + (TI_SW + 2), u_lo[:, 8 + m.odd, :], u_hi[:, 8 + m.odd, :])

            def sw_step(m, before=True, dense=True):
                p = m + -1
                for n in range(4):
                    sw_logits(p, n)
                    if n == 0:
                        split_weights(m + (CH_SW + 5))
                    if n == 3 and dense:
                        queries_low(m)
                    if n == 1 and before:
                        sw_o_low(p + -1, 1)
                    if n == 3:
                        sw_o_low(p, 0)
                    if n == 2 and dense:
                        scale_queries(m)
                    if before or n >= 1:
                        sw_pt_low(*sw_unit_by(p, n, -1))
                    sw_scale_probs(p, n)
                    if n == 3 and not dense:
                        split_weights(m + (CH_SW + 6))

            nc.vector.memset(ones[:], 1.0).then_inc(filled, 1)
            nc.vector.memset(eps[:], EPS).then_inc(filled, 1)
            clear_squares(0)
            split_weights(At(0))
            dve.wait_ge(gain_landed, 16)
            for k in range(KT):
                finish_x(0, At(k))
                if k == 5:
                    split_weights(At(1))
            na_step(At(0), attend=False)
            dve.wait_ge(consts_landed, 16 * 2)
            nc.vector.tensor_scalar(nsink[:], sink[:], -1.0, None, ALU.mult).then_inc(nsink_made, 1)
            na_step(At(1))
            with dve.Fori(0, 3) as i:
                for n in range(2):
                    na_step(At(2 + n, 2, i))
            na_step(At(8), dense=False)
            nc.vector.memset(t5_row, LOWEST).then_inc(t5_cleared, 1)
            dve.wait_ge(t5_cleared, 1)
            dve.wait_ge(t5_product, 1)
            nc.vector.tensor_copy(t5_row[:, P - 1:P - 1 + RELS], flat(misc_ps[:])[0:HEADS, 0:RELS]).then_inc(t5_made, 1)
            clear_squares(1)
            output_projection(CH_NAO, GR_NAO, 1)
            mlp(CH_MLP0, GR_MLP0, TI_MLP0, 1)
            reciprocal_deviation(2)
            scale_tile(At(CH_SW), At(GR_SW), At(TI_SW), 1.0)
            split_weights(At(CH_SW + 2))
            tile_low(At(TI_SW), k_lo[:, 0, :], k_hi[:, 0, :])
            dve.wait_ge(t5_stored, 16 * QC)
            scale(At(CH_SW + 1), At(GR_SW + 1), vT[:, :], 1.0)
            split_weights(At(CH_SW + 3))
            scale_tile(At(CH_SW + 2), At(GR_SW + 2), At(TI_SW + 1), 1.0)
            split_weights(At(CH_SW + 4))
            tile_low(At(TI_SW + 1), k_lo[:, 1, :], k_hi[:, 1, :])
            v_low(At(UNITS_NA), slice(0, 4))
            dve.wait_ge(vt_done, UNITS_NA + 1)
            scale(At(CH_SW + 3), At(GR_SW + 3), vT[:, :], 1.0)
            split_weights(At(CH_SW + 5))
            scale_queries(At(0))
            queries_low(At(0))
            v_low(At(UNITS_NA + 1), slice(4, 8))
            sw_step(At(1), before=False)
            with dve.Fori(0, 3) as i:
                for n in range(2):
                    sw_step(At(2 + n, 2, i))
            sw_step(At(8), dense=False)
            sw_pt_low(At(7), 3)
            split_weights(At(CH_SWO + 3))
            sw_o_low(At(7), 1)
            clear_squares(3)
            output_projection(CH_SWO, GR_SWO, 3)
            mlp(CH_MLP1, GR_MLP1, TI_MLP1, 3)
            reciprocal_deviation(4)
            for k in range(KT):
                nc.vector.scalar_tensor_tensor(out=x[:, k, :], in0=x[:, k, :],
                                               scalar=gain[:, 4 * KT + k:4 * KT + k + 1], in1=rstd[:],
                                               op0=ALU.mult, op1=ALU.mult).then_inc(y_made, 1)



def blocks_of(w):
    k, m = w.shape
    t = w.reshape(k // P, P, m // P, P).transpose(2, 0, 1, 3).reshape(-1, BLOCKS, P, P)
    return t.transpose(0, 2, 1, 3).reshape(-1, P, CHUNK)


def projection_blocks(w):
    t = w.reshape(KT, P, KT, P).transpose(2, 0, 1, 3)
    early = np.stack([t[g, k] for g, k in EARLY_BLOCKS]).reshape(EARLY, BLOCKS, P, P)
    return np.concatenate([early.transpose(0, 2, 1, 3).reshape(-1, P, CHUNK), blocks_of(w[:, EARLY * P:])])


def sw_heads():
    return [8 * (t % 2) + 4 * hh + t // 2 for t in range(PAIRS) for hh in range(2)]


def mask_constant():
    col = np.arange(COLS)
    start = np.clip(col - NA_COLS // 2, 0, COLS - NA_COLS)
    m = np.full((ROWS, QC, QT, WC), LOWEST, np.float32)
    for j in range(QT):
        for q in range(QC):
            key = WIN0[j] + np.arange(WC)
            s = start[QC * j + q]
            m[:, q, j, (key >= s) & (key < s + NA_COLS)] = 0.0
    return m.reshape(P, QT, WC)


def onehot_constant():
    buckets, exact, farthest = 32, 8, 128
    half = buckets // 2
    rel = np.arange(-P, P + 1)
    n = np.abs(rel)
    nf = np.maximum(n, 1).astype(np.float32)
    large = exact + (np.log(nf / np.float32(exact)) / np.float32(np.log(farthest / exact))
                     * np.float32(half - exact)).astype(np.int32)
    bucket = np.where(rel > 0, half, 0) + np.where(n < exact, n, np.minimum(large, half - 1))
    return (bucket[None, :] == np.arange(buckets)[:, None]).astype(np.float32)


def kernel(x, mix_norm, mlp_norm, final_norm, na_w_qkv, na_rpb, na_w_o, swa_w_qkv, swa_sinks, swa_w_o,
           t5_rel_table, mlp_w_in, mlp_w_out):
    import concourse.bacc as bacc
    from concourse.bass_utils import run_bass_kernel_spmd

    arr = np.asarray
    na, sw = arr(na_w_qkv)[0], arr(swa_w_qkv)[0]
    na_qkv = na.reshape(D, 3, KT, P).transpose(0, 2, 1, 3).reshape(D, 3 * D)
    heads = sw_heads()
    sw_q = sw[:, :D].reshape(D, HEADS, HD)[:, heads].reshape(D, D)
    sw_k, sw_v = sw[:, D:D + KV * HD], sw[:, D + KV * HD:]
    sw_kv = np.concatenate([sw_k[:, :P], sw_v[:, :P], sw_k[:, P:], sw_v[:, P:]], axis=1)
    sw_o = arr(swa_w_o)[0].reshape(HEADS, HD, D)[heads].reshape(D, D)
    w_in, w_out = arr(mlp_w_in), arr(mlp_w_out)

    def mlp_chunks(n):
        out = []
        for half in range(2):
            s = slice(FF // 2 * half, FF // 2 * (half + 1))
            out += [blocks_of(w_in[n][:, s]), blocks_of(w_out[n][s])]
        return out

    stream = np.concatenate([blocks_of(na_qkv), projection_blocks(arr(na_w_o)[0]), *mlp_chunks(0), blocks_of(sw_kv),
                             blocks_of(sw_q), projection_blocks(sw_o), *mlp_chunks(1)])
    mix, mlp = arr(mix_norm), arr(mlp_norm)
    gains = np.stack([mix[0], mlp[0], mix[1], mlp[1], arr(final_norm)])
    arrays = {
        "in_xT": arr(x)[0].T.reshape(KT, P, SEQ),
        "in_wstream": stream,
        "in_gains": gains.reshape(NORMS * KT, P).T,
        "in_rpb": arr(na_rpb)[0],
        "in_sinks": arr(swa_sinks)[0][heads],
        "in_rel_table": arr(t5_rel_table)[:, heads],
        "in_mask": mask_constant(),
        "in_onehot": onehot_constant(),
    }
    arrays = {k: np.ascontiguousarray(a) for k, a in arrays.items()}
    nc = bacc.Bacc("TRN2", target_bir_lowering=False, num_devices=1)
    args = [nc.dram_tensor(k, a.shape, mybir.dt.from_np(a.dtype), kind="ExternalInput").ap()
            for k, a in arrays.items()]
    out = nc.dram_tensor("out_y", (KT, P, SEQ), F32, kind="ExternalOutput").ap()
    encoder(nc, *args, out)
    r = run_bass_kernel_spmd(nc, [arrays], core_ids=[0])
    return np.ascontiguousarray(arr(r.results[0]["out_y"]).reshape(D, SEQ).T).reshape(1, SEQ, D)
```
